# Optimizing a Trainium2 kernel written in Bass

```python
import math
import jax, jax.numpy as jnp
from jax import lax
import numpy as np

D_MODEL = 1024
BATCH = 1
SEQ = 128
DEPTH = 2
DEC_BATCH = 1
DEC_SEQ = 256
PAST_LEN = 128

GRID_W = 64
D_CONV = 512
CONV_WIDTH = 31
N_HEADS_B = 4
HEAD_DIM_B = 64
D_ATTN = N_HEADS_B * 2 * HEAD_DIM_B
D_IN_EVEN = 2 * D_CONV + 3 * D_ATTN
D_MIX_OUT = D_CONV + D_ATTN
N_FOURIER_GROUPS = 4
N_EXPERT_GROUPS = 4
EXPERTS_PER_GROUP = 4
N_EXPERTS = N_EXPERT_GROUPS * EXPERTS_PER_GROUP
TOP_K_IN_GROUP = 2
D_EXPERT = 512
ROPE_BASE = 10000.0
Q_BLOCK = 128
N_ATTN_LAYERS = (DEPTH + 1) // 2
N_FOURIER_LAYERS = DEPTH // 2
EPS = 1e-6

kernel_name = 'hybrid_diffusion_conv_diffattn_fnet_hmoe_step'

def rms_norm(x, g):
    xf = x.astype(jnp.float32)
    y = xf * lax.rsqrt(jnp.mean(xf * xf, axis=-1, keepdims=True) + EPS)
    return (y * g.astype(jnp.float32)).astype(x.dtype)

def layer_norm(x, g, b):
    xf = x.astype(jnp.float32)
    mu = jnp.mean(xf, axis=-1, keepdims=True)
    var = jnp.mean(jnp.square(xf - mu), axis=-1, keepdims=True)
    y = (xf - mu) * lax.rsqrt(var + EPS)
    return (y * g.astype(jnp.float32) + b.astype(jnp.float32)).astype(x.dtype)

def ada_params(cond, w_mod_l, b_mod_l):
    m = jax.nn.silu(cond) @ w_mod_l + b_mod_l
    return jnp.split(m, 6, axis=-1)

def modulate(h, shift, scale):
    return h * (1 + scale[:, None, :]) + shift[:, None, :]

def axial_rope(x):
    S = x.shape[1]
    rows = S // GRID_W
    r, col = jnp.meshgrid(jnp.arange(rows, dtype=jnp.float32), jnp.arange(GRID_W, dtype=jnp.float32), indexing='ij')
    r, col = r.reshape(-1), col.reshape(-1)
    half = HEAD_DIM_B // 2
    n_freq = half // 2
    inv = ROPE_BASE ** (-jnp.arange(n_freq, dtype=jnp.float32) / n_freq)

    def rot(xs, pos):
        ang = pos[:, None] * inv[None, :]
        cos = jnp.cos(ang)[None, :, None, None, :].astype(x.dtype)
        sin = jnp.sin(ang)[None, :, None, None, :].astype(x.dtype)
        x1, x2 = xs[..., :n_freq], xs[..., n_freq:]
        return jnp.concatenate([x1 * cos - x2 * sin, x1 * sin + x2 * cos], axis=-1)

    return jnp.concatenate([rot(x[..., :half], r), rot(x[..., half:], col)], axis=-1)

def depthwise_conv(z, w, b):
    C = z.shape[-1]
    y = lax.conv_general_dilated(z, w[:, None, :].astype(z.dtype), (1,), [(CONV_WIDTH // 2, CONV_WIDTH // 2)],
                                 dimension_numbers=('NWC', 'WIO', 'NWC'), feature_group_count=C)
    return y + b

def diff_attention(q, k, v, lam):
    B, Lq = q.shape[0], q.shape[1]
    nb = Lq // Q_BLOCK
    qb = jnp.moveaxis(q.reshape(B, nb, Q_BLOCK, N_HEADS_B, 2, HEAD_DIM_B), 1, 0)
    scale = HEAD_DIM_B ** -0.5

    def block(qblk):
        s = jnp.einsum('bqhcd,bkhcd->bchqk', qblk, k).astype(jnp.float32) * scale
        p = jax.nn.softmax(s, axis=-1)
        w = p[:, 0] - lam * p[:, 1]
        return jnp.einsum('bhqk,bkhe->bqhe', w.astype(v.dtype), v)

    o = lax.map(block, qb)
    return jnp.moveaxis(o, 0, 1).reshape(B, Lq, N_HEADS_B, 2 * HEAD_DIM_B)

def even_mixer(h, w_in, w_out, conv_w, conv_b, ln_g, ln_b, subln_g, lam, lam_init, ctx_k=None, ctx_v=None):
    B, L, _ = h.shape
    p = h @ w_in
    o0 = 2 * D_CONV
    u = p[..., :o0]
    q = p[..., o0:o0 + D_ATTN].reshape(B, L, N_HEADS_B, 2, HEAD_DIM_B)
    k = p[..., o0 + D_ATTN:o0 + 2 * D_ATTN].reshape(B, L, N_HEADS_B, 2, HEAD_DIM_B)
    v = p[..., o0 + 2 * D_ATTN:].reshape(B, L, N_HEADS_B, 2 * HEAD_DIM_B)
    a, gate = jnp.split(u, 2, axis=-1)
    z = a * jax.nn.sigmoid(gate)
    z = jax.nn.silu(layer_norm(depthwise_conv(z, conv_w, conv_b), ln_g, ln_b))
    if ctx_k is None:
        o = diff_attention(q, k, v, lam)
    else:
        Lc = ctx_k.shape[1]
        k_all = jnp.concatenate([ctx_k.reshape(B, Lc, N_HEADS_B, 2, HEAD_DIM_B), axial_rope(k)], axis=1)
        v_all = jnp.concatenate([ctx_v, v], axis=1)
        o = diff_attention(axial_rope(q), k_all, v_all, lam)
    o = rms_norm(o, subln_g) * (1.0 - lam_init)
    out = jnp.concatenate([z, o.reshape(B, L, D_ATTN)], axis=-1) @ w_out
    return out, k.reshape(B, L, N_HEADS_B, 2 * HEAD_DIM_B), v

def fourier_mix(h, w):
    B, L, D = h.shape
    z = h.astype(jnp.float32).reshape(B, L, N_FOURIER_GROUPS, D // N_FOURIER_GROUPS)
    f = jnp.fft.fftn(z, axes=(1, 3), norm='ortho').real.astype(h.dtype).reshape(B, L, D)
    return f @ w

def hier_moe(h, w_rg, b_rg, w_re, b_re, w_gate, w_up, w_down):
    B, L, D = h.shape
    x = h.reshape(-1, D)
    N = x.shape[0]
    g_prob = jax.nn.softmax((x @ w_rg + b_rg).astype(jnp.float32), axis=-1)
    g_p, g_idx = lax.top_k(g_prob, 1)
    e_logits = (x @ w_re + b_re).astype(jnp.float32).reshape(N, N_EXPERT_GROUPS, EXPERTS_PER_GROUP)
    e_sel = jnp.take_along_axis(e_logits, g_idx[:, :, None], axis=1)[:, 0]
    e_p, e_idx = lax.top_k(jax.nn.softmax(e_sel, axis=-1), TOP_K_IN_GROUP)
    weights = g_p * e_p / jnp.sum(e_p, axis=-1, keepdims=True)
    expert_id = g_idx * EXPERTS_PER_GROUP + e_idx
    combine = jnp.sum(jax.nn.one_hot(expert_id, N_EXPERTS, dtype=jnp.float32) * weights[..., None], axis=1)
    hid = jax.nn.silu(jnp.einsum('nd,edf->nef', x, w_gate)) * jnp.einsum('nd,edf->nef', x, w_up)
    hid = hid * combine[:, :, None].astype(hid.dtype)
    return jnp.einsum('nef,efd->nd', hid, w_down).reshape(B, L, D)

def setup_inputs(seed: int = 0) -> dict:
    key = jax.random.key(seed)
    ks = jax.random.split(key, 32)
    f32 = jnp.float32

    def nrm(k, shape, scale=1.0):
        return jax.random.normal(k, shape, f32) * scale

    hd2 = 2 * HEAD_DIM_B
    return {
        'x_prompt': nrm(ks[0], (BATCH, SEQ, D_MODEL)),
        'x_sample': nrm(ks[1], (DEC_BATCH, DEC_SEQ, D_MODEL)),
        'cache_k': nrm(ks[2], (DEC_BATCH, N_ATTN_LAYERS, PAST_LEN, N_HEADS_B, hd2)),
        'cache_v': nrm(ks[3], (DEC_BATCH, N_ATTN_LAYERS, PAST_LEN, N_HEADS_B, hd2)),
        'c': nrm(ks[4], (DEC_BATCH, D_MODEL)),
        'c_ctx': nrm(ks[5], (D_MODEL,)),
        'w_mod': nrm(ks[6], (DEPTH, D_MODEL, 6 * D_MODEL), 0.5 * D_MODEL ** -0.5),
        'b_mod': nrm(ks[7], (DEPTH, 6 * D_MODEL), 0.02),
        'norm1_g': 1.0 + nrm(ks[8], (DEPTH, D_MODEL), 0.05),
        'norm2_g': 1.0 + nrm(ks[9], (DEPTH, D_MODEL), 0.05),
        'w_in_even': nrm(ks[10], (N_ATTN_LAYERS, D_MODEL, D_IN_EVEN), D_MODEL ** -0.5),
        'conv_w': nrm(ks[11], (N_ATTN_LAYERS, CONV_WIDTH, D_CONV), CONV_WIDTH ** -0.5),
        'conv_b': nrm(ks[12], (N_ATTN_LAYERS, D_CONV), 0.02),
        'conv_ln_g': 1.0 + nrm(ks[13], (N_ATTN_LAYERS, D_CONV), 0.05),
        'conv_ln_b': nrm(ks[14], (N_ATTN_LAYERS, D_CONV), 0.02),
        'lambda_q1': nrm(ks[15], (N_ATTN_LAYERS, HEAD_DIM_B), 0.1),
        'lambda_k1': nrm(ks[16], (N_ATTN_LAYERS, HEAD_DIM_B), 0.1),
        'lambda_q2': nrm(ks[17], (N_ATTN_LAYERS, HEAD_DIM_B), 0.1),
        'lambda_k2': nrm(ks[18], (N_ATTN_LAYERS, HEAD_DIM_B), 0.1),
        'subln_g': 1.0 + nrm(ks[19], (N_ATTN_LAYERS, hd2), 0.05),
        'w_out_even': nrm(ks[20], (N_ATTN_LAYERS, D_MIX_OUT, D_MODEL), D_MIX_OUT ** -0.5),
        'w_fnet': nrm(ks[21], (N_FOURIER_LAYERS, D_MODEL, D_MODEL), D_MODEL ** -0.5),
        'w_router_group': nrm(ks[22], (DEPTH, D_MODEL, N_EXPERT_GROUPS), D_MODEL ** -0.5),
        'b_router_group': nrm(ks[23], (DEPTH, N_EXPERT_GROUPS), 0.01),
        'w_router_expert': nrm(ks[24], (DEPTH, D_MODEL, N_EXPERTS), D_MODEL ** -0.5),
        'b_router_expert': nrm(ks[25], (DEPTH, N_EXPERTS), 0.01),
        'w_gate_exp': nrm(ks[26], (DEPTH, N_EXPERTS, D_MODEL, D_EXPERT), D_MODEL ** -0.5),
        'w_up_exp': nrm(ks[27], (DEPTH, N_EXPERTS, D_MODEL, D_EXPERT), D_MODEL ** -0.5),
        'w_down_exp': nrm(ks[28], (DEPTH, N_EXPERTS, D_EXPERT, D_MODEL), D_EXPERT ** -0.5),
        'final_norm_g': 1.0 + nrm(ks[29], (D_MODEL,), 0.05),
    }

def reference(x_prompt, x_sample, cache_k, cache_v, c, c_ctx, w_mod, b_mod, norm1_g, norm2_g,
              w_in_even, conv_w, conv_b, conv_ln_g, conv_ln_b, lambda_q1, lambda_k1, lambda_q2, lambda_k2,
              subln_g, w_out_even, w_fnet, w_router_group, b_router_group, w_router_expert, b_router_expert,
              w_gate_exp, w_up_exp, w_down_exp, final_norm_g):
    y_p = x_prompt
    y_s = x_sample
    new_k, new_v = [], []
    for l in range(DEPTH):
        j = l // 2
        sh1p, sc1p, g1p, sh2p, sc2p, g2p = ada_params(c_ctx[None, :], w_mod[l], b_mod[l])
        sh1s, sc1s, g1s, sh2s, sc2s, g2s = ada_params(c, w_mod[l], b_mod[l])
        hp = modulate(rms_norm(y_p, norm1_g[l]), sh1p, sc1p)
        hs = modulate(rms_norm(y_s, norm1_g[l]), sh1s, sc1s)
        if l % 2 == 0:
            lam_init = 0.8 - 0.6 * math.exp(-0.3 * l)
            lam = (jnp.exp(jnp.sum(lambda_q1[j].astype(jnp.float32) * lambda_k1[j].astype(jnp.float32)))
                   - jnp.exp(jnp.sum(lambda_q2[j].astype(jnp.float32) * lambda_k2[j].astype(jnp.float32)))
                   + lam_init)
            args = (w_in_even[j], w_out_even[j], conv_w[j], conv_b[j], conv_ln_g[j], conv_ln_b[j], subln_g[j], lam, lam_init)
            op, kp, vp = even_mixer(hp, *args)
            os_, _, _ = even_mixer(hs, *args, ctx_k=cache_k[:, j], ctx_v=cache_v[:, j])
            new_k.append(kp)
            new_v.append(vp)
        else:
            op = fourier_mix(hp, w_fnet[j])
            os_ = fourier_mix(hs, w_fnet[j])
        y_p = y_p + g1p[:, None, :] * op
        y_s = y_s + g1s[:, None, :] * os_
        moe_args = (w_router_group[l], b_router_group[l], w_router_expert[l], b_router_expert[l],
                    w_gate_exp[l], w_up_exp[l], w_down_exp[l])
        y_p = y_p + g2p[:, None, :] * hier_moe(modulate(rms_norm(y_p, norm2_g[l]), sh2p, sc2p), *moe_args)
        y_s = y_s + g2s[:, None, :] * hier_moe(modulate(rms_norm(y_s, norm2_g[l]), sh2s, sc2s), *moe_args)
    y_prompt = rms_norm(y_p, final_norm_g)
    y_sample = rms_norm(y_s, final_norm_g)
    new_cache_k = jnp.stack(new_k, axis=1)
    new_cache_v = jnp.stack(new_v, axis=1)
    return (y_prompt, y_sample, new_cache_k, new_cache_v)


_drawn_inputs = setup_inputs


def setup_inputs(seed=0):
    import zlib

    import numpy as np

    out = dict(_drawn_inputs(seed))
    spreads = {}
    factors = {'conv_b': 5.617,
     'conv_ln_g': 4.393,
     'conv_ln_b': 24.167,
     'lambda_q1': 4.291,
     'lambda_k1': 5.731,
     'lambda_q2': 5.177,
     'lambda_k2': 8.0,
     'subln_g': 5.089,
     'b_router_group': 21.013,
     'b_router_expert': 39.067,
     'norm2_g': 3.679}
    for name, (base, spread) in spreads.items():
        noise = np.random.default_rng([zlib.crc32(name.encode()), seed]).standard_normal(out[name].shape)
        drawn = base * np.exp(spread * noise) if base else spread * noise
        out[name] = __import__('jax').numpy.asarray(drawn.astype(out[name].dtype))
    for name, factor in factors.items():
        out[name] = (out[name] * factor).astype(out[name].dtype)
    return out
```

```python
import numpy as np
import concourse.bass as bass
from concourse import mybir
from contextlib import ExitStack

D = 1024
TOK = 384
TB = 3
NE = 16
SLOTS = 2 * TOK
F = 512
UNIT = 2048
RAW, SPL = 6, 3
PAD = 15
TAPS = 31
ZS = 2 * PAD + 128
ZL = ZS + 256 + PAD
CL = ZL - 2 * PAD
EPS = 1e-6
BIG = 100000.0

MOD0, WIN, WOUT, MOE0, WF, MOE1, END = 0, 12, 22, 26, 122, 126, 222
PLAIN = 36


def ring(g):
    return g + (PLAIN if g >= WOUT else 0)



C_ID, C_TRI, C_ONE = 0, 128, 256
C_COS, C_SIN = 384, 448
C_J4, C_J16 = 512, 516
C_EP = 548
C_P = 599
C_HALF = 602
C_SC = 618
C_N = 619


def constants():
    c = np.zeros((128, C_N), np.float32)
    p = np.arange(128)
    c[:, C_ID:C_ID + 128] = np.eye(128)
    c[:, C_TRI:C_TRI + 128] = p[:, None] < p[None, :]
    c[:, C_ONE:C_ONE + 128] = 1.0
    inv = (np.float32(10000.0) ** (-np.arange(16, dtype=np.float32) / np.float32(16))).astype(np.float32)
    for b in range(2):
        j = 128 * b + p
        for half, pos in enumerate((j // 64, j % 64)):
            ang = pos.astype(np.float32)[:, None] * inv[None, :]
            o = (2 * b + half) * 16
            c[:, C_COS + o:C_COS + o + 16] = np.cos(ang)
            c[:, C_SIN + o:C_SIN + o + 16] = np.sin(ang)
    c[:, C_J4:C_J4 + 4] = np.arange(4) - 4
    c[:, C_J16:C_J16 + 16] = np.arange(16) - 16
    for b in range(3):
        c[:, C_EP + 17 * b:C_EP + 17 * b + 16] = (128 * b + p)[:, None]
        c[:, C_EP + 17 * b + 16] = BIG
        c[:, C_P + b] = p + 128 * b
    c[:, C_HALF:C_HALF + 16] = -0.5
    c[:, C_SC] = (p < 48) & (p % 24 // 8 == 1)
    return c


def dft_tables():
    t = np.zeros((128, 2304), np.float64)
    p = np.arange(128)

    def ang(rows, n):
        return 2 * np.pi * ((rows[:, None] * np.arange(n)[None, :]) % n) / n

    a = ang(p, 128)
    s = 1 / np.sqrt(128 * 256)
    t[:, 0:128], t[:, 128:256] = np.cos(a) * s, np.sin(a) * s
    s = 1 / np.sqrt(256 * 256)
    for j in range(2):
        a = ang(p + 128 * j, 256)
        t[:, 256 + 512 * j:512 + 512 * j], t[:, 512 + 512 * j:768 + 512 * j] = np.cos(a) * s, np.sin(a) * s
        t[:, 1280 + 256 * j:1536 + 256 * j], t[:, 1792 + 256 * j:2048 + 256 * j] = np.cos(a), -np.sin(a)
    return t.astype(np.float32)


def build(nc, x_prompt, x_sample, cache_k, cache_v, c, c_ctx, w_mod, b_mod, norm1_g, norm2_g, w_in_even,
          conv_w, conv_b, conv_ln_g, conv_ln_b, lambda_q1, lambda_k1, lambda_q2, lambda_k2, subln_g,
          w_out_even, w_fnet, w_router_group, b_router_group, w_router_expert, b_router_expert,
          w_gate_exp, w_up_exp, w_down_exp, final_norm_g, consts, dft,
          y_prompt, y_sample, new_k, new_v):
    f32, f32r, i32 = mybir.dt.float32, mybir.dt.float32r, mybir.dt.int32
    ACT, ALU, AX = mybir.ActivationFunctionType, mybir.AluOpType, mybir.AxisListType
    ds = bass.ds
    ctx = ExitStack()
    with ctx:
        def sem(name):
            return ctx.enter_context(nc.semaphore(name))

        at = [16512]

        def place(name, words, dt=f32, shape=None, over=None):
            off = over if over is not None else at[0]
            if over is None:
                at[0] += -(-4 * words // 32) * 32
            return nc.alloc_sbuf_tensor_at(name, [128] + list(shape or [words]), dt, offset=off)

        raw = place("raw", RAW * UNIT, f32, [RAW, UNIT])
        H = place("H", SPL * UNIT, f32r, [SPL, UNIT])
        L = place("L", SPL * UNIT, f32r, [SPL, UNIT])
        y = place("y", 3 * D, f32, [3, D])
        o_h = at[0]
        h = place("h", 3 * D, f32, [3, D])
        o_th, o_tl = at[0], at[0] + 12 * D
        hTh = place("hTh", 3 * D, f32r, [8, TOK])
        hTl = place("hTl", 3 * D, f32r, [8, TOK])
        modrow = place("modrow", 3 * D, over=o_th)
        kT = place("kT", 2048, f32, [4, 512], over=o_th)
        pA = place("pA", 768, f32, [2, 384], over=o_th + 8192)
        qT = place("qT", 1536, f32, [4, TOK], over=o_tl)
        wT = place("wT", 768, f32, [2, 384], over=o_tl + 6144)
        pB = place("pB", 768, f32, [2, 384], over=o_tl + 9216)
        o_par = at[0]
        par = place("par", 6 * D, f32, [3, 2, D])
        bmod = place("bmod", 3 * D, over=o_par)
        cat = place("cat", 3 * D, f32, [3, D], over=o_par)
        ck = place("ck", 512, over=o_par + 12 * D)
        cv = place("cv", 512, over=o_par + 12 * D + 2048)
        wov = place("wov", 2 * UNIT, f32, [2, UNIT], over=o_par)
        o_s = at[0]
        vt = place("vt", 1536, f32, [3, 512])
        zpad = place("zpad", 4 * ZL, f32, [4, ZL])
        o_conv = at[0]
        conv = place("conv", 4 * CL, f32, [4, CL])
        sig = place("sig", 768, f32, [2, TOK])
        end_s = at[0]
        rtmp = place("rtmp", 2048, f32, [4, 512], over=o_conv)
        tmp3 = place("tmp3", 768, f32, [3, 256], over=o_s)
        gn = place("gn", D, over=o_h)
        xg = place("xg", 1024, over=o_s)
        sg = place("sg", 512, over=o_s + 4096)
        hid = place("hid", 512, over=o_s + 6144)
        yrow = place("yrow", 1024, over=o_s + 8192)
        ga = place("ga", 1024, over=o_s + 12288)
        gb = place("gb", 1024, over=o_s + 16384)
        xTo = place("xTo", 1024, f32, [8, 128], over=o_s + 12288)
        hTo = place("hTo", 512, f32, [4, 128], over=o_s + 16384)
        P = place("P", 3072, f32, [2, 2, 768], over=o_s)
        dftt = place("dftt", 2304, over=o_s + 12288)
        assert o_s + 12288 + 9216 <= end_s
        cst = place("cst", C_N)
        cT = place("cT", 16, f32, [2, 8])
        cS = place("cS", 16, f32, [8, 2])
        cH = place("cH", 16, f32r, [8, 2])
        cL = place("cL", 16, f32r, [8, 2])
        o_cwr = at[0]
        cwr = place("cwr", 512)
        mrow2 = place("mrow2", 512, f32, [2, 256], over=o_cwr)
        cw = place("cw", 128, f32, [4, 32])
        lnb = place("lnb", 1024, f32, [2, 512])
        o_lamv = at[0]
        lamv = place("lamv", 256, f32, [4, 64])
        mbias = place("mbias", 128, over=o_lamv)
        mgain = place("mgain", 128, over=o_lamv + 512)
        mset = place("mset", 128)
        lams = place("lams", 8)
        sub = place("sub", 128)
        wr = place("wr", 160, f32, [8, 20])
        wrh = place("wrh", 160, f32r, [8, 20])
        wrl = place("wrl", 160, f32r, [8, 20])
        brt = place("brt", 40, f32, [2, 20])
        small = place("small", 160)
        rt = place("rt", 720)
        di = place("di", 8, i32)
        gtab = place("gtab", 52, i32)
        gix = place("gix", 8, i32)
        six = place("six", 8, i32)
        mxi = place("mxi", 8, i32)
        assert at[0] <= 229344, at[0]
        ps = ctx.enter_context(nc.psum_tensor("ps", [128, 8, 512], f32))
        ident = cst[:, C_ID:C_ID + 128]

        modd = nc.dram_tensor("modd", [4, 2, 3, D], f32).ap()
        modx = nc.dram_tensor("modx", [3, 2, 3 * D], f32).ap()
        xs = nc.dram_tensor("xs", [SLOTS, D], f32).ap()
        ysl = nc.dram_tensor("ysl", [SLOTS, D], f32).ap()

        s_raw = [sem(f"raw_loaded{i}") for i in range(RAW)]
        s_hi, s_lo, s_unit = sem("unit_rounded"), sem("unit_split"), sem("unit_used")
        s_cst, s_small, s_yin, s_cT = sem("consts_in"), sem("small_in"), sem("y_in"), sem("cond_in")
        s_bmod, s_gn = sem("bmod_in"), sem("gains_in")
        s_sil, s_cs = sem("cond_silu"), sem("cond_split")
        s_mev, s_mrow, s_mst, s_par = sem("mod_evac"), sem("mod_row"), sem("mod_stored"), sem("par_in")
        s_gate, s_plain, s_pev = sem("gates_in"), sem("plain_used"), sem("plain_evac")
        s_mxs, s_mset, s_mdone = [sem(f"products_stored{i}") for i in range(2)], sem("set_in"), sem("set_done")
        s_sq, s_rstd, s_h = sem("sq_sum"), sem("rstd"), sem("h_ready")
        s_tp, s_th, s_tl = sem("transposed"), sem("t_hi"), sem("t_lo")
        s_sig, s_z, s_qkv = sem("sigmoid"), sem("glu"), sem("qkv_out")
        s_zp, s_rope = sem("pads_zero"), sem("rope")
        s_cwt, s_cw = sem("taps_transposed"), sem("taps_ready")
        s_cach, s_kv = sem("cache_in"), sem("kv_stored")
        s_atp, s_aT, s_sc, s_nm, s_p = sem("qk_transposed"), sem("qk_T"), sem("scores"), sem("neg_max"), sem("probs")
        s_w, s_wtp, s_wT, s_pv, s_o = sem("weights"), sem("w_transposed"), sem("w_T"), sem("pv"), sem("o_out")
        s_lam, s_le, s_rso, s_on = sem("lam_dots"), sem("lam_exp"), sem("o_rstd"), sem("o_normed")
        s_tap = sem("taps_added")
        s_conv, s_ztp, s_zv, s_rsz, s_zn, s_zs = (sem("conv_done"), sem("z_transposed"), sem("z_var"), sem("z_rstd"),
                                                 sem("z_normed"), sem("z_silu"))
        s_yo, s_y = sem("proj_added"), sem("y_ready")
        s_wrin, s_wrh, s_wrl, s_lg = sem("router_in"), sem("router_hi"), sem("router_lo"), sem("logits")
        s_rg, s_re, s_sel, s_cum, s_route = sem("gate_in"), sem("gate_exp"), sem("selected"), sem("counted"), sem("routed")
        s_xsc, s_gi, s_xg, s_xtp, s_xth, s_xtl = (sem("x_scattered"), sem("idx_ready"), sem("x_gathered"),
                                                 sem("x_transposed"), sem("x_hi"), sem("x_lo"))
        s_sg, s_hid, s_htp, s_hth, s_htl = sem("silu_gate"), sem("hidden"), sem("hid_transposed"), sem("hid_hi"), sem("hid_lo")
        s_yev, s_ysc = sem("y_evac"), sem("y_scattered")
        s_rd, s_re2 = sem("top2_diff"), sem("top2_exp")
        s_ga, s_gu = sem("pair_gathered"), sem("pair_used")
        s_dft, s_s1, s_Pa, s_Pd, s_s2 = sem("dft_in"), sem("dft_stage1"), sem("P_act"), sem("P_dve"), sem("dft_stage2")
        s_fh, s_fl = sem("f_hi"), sem("f_lo")
        s_out, s_hold = sem("out_stored"), sem("pool_held")
        s_dch, s_pch, s_ach = sem("dve_chain"), sem("pool_chain"), sem("act_chain")
        OV = [{n: sem(f"ov{l}_{n}") for n in ("g", "i", "u", "tp", "xt", "sg", "hid", "htp", "ht", "y", "st")}
              for l in range(2)]
        for l in range(2):
            OV[l]["w"] = [sem(f"ov{l}_w{i}") for i in range(2)]

        wexp = [t.rearrange("l e (p k) n -> l e p (k n)", p=128) for t in (w_gate_exp, w_up_exp, w_down_exp)]

        def expert_src(l, e, u):
            return wexp[u // 2][l, ds(e, 1), :, (u % 2) * UNIT:(u % 2 + 1) * UNIT].rearrange("a p n -> p (a n)")

        block = ctx.enter_context(nc.Block())

        @block.sync
        def _(sp):
            def load(r, src, k=None, i=None):
                if r >= RAW:
                    q = r - RAW
                    if q < WOUT:
                        done, n = s_lo, q + 1
                    elif q < WOUT + PLAIN:
                        done, n = s_plain, q - WOUT + 1
                    else:
                        done, n = s_lo, q - PLAIN + 1
                    sp.wait_ge(done, n if i is None else i * 6 + n)
                dst = raw[:, r % RAW, :]
                sp.dma_start(dst.rearrange("p (k n) -> p k n", k=k) if k else dst, src).then_inc(s_raw[r % RAW], 16)

            def mod_src(l, col):
                return w_mod[l].rearrange("(p k) n -> p k n", p=128)[:, :, col]

            def overflow_loads(l):
                O = OV[l]
                sp.wait_ge(s_route, l + 1)
                cnt = sp.value_load(mxi[0:1, 0:1], min_val=0, max_val=TOK)
                with sp.If(cnt > 128):
                    for b in (1, 2):
                        with sp.Fori(0, NE) as e:
                            for u in range(6):
                                n0 = 6 * NE * (b - 1)
                                if u == 0:
                                    sp.wait_ge(O["i"], e + (17 * (b - 1) + 1))
                                if u >= 2:
                                    sp.wait_ge(O["u"], e * 6 + (n0 + u - 1))
                                sp.dma_start(wov[:, u % 2, :], expert_src(l, e, u)).then_inc(O["w"][u % 2], 16)

            for u in range(12):
                load(u, mod_src(0, slice(256 * u, 256 * u + 256)), k=8)
            win = w_in_even[0].rearrange("(p k) n -> p k n", p=128)
            for j, col in enumerate((2, 0, 3, 1, 4, 5, 6, 7, 8, 9)):
                load(WIN + j, win[:, :, 256 * col:256 * col + 256], k=8)
            for u in range(12):
                load(WOUT + u, mod_src(0, slice(3 * D + 256 * u, 3 * D + 256 * u + 256)), k=8)
            with sp.Fori(0, 4) as i:
                for u in range(6):
                    load(WOUT + 12 + u, mod_src(1, ds(i * 1536 + 256 * u, 256)), k=8, i=i)
            wout = w_out_even[0].rearrange("(p k) n -> p k n", p=128)
            for j in range(4):
                load(ring(WOUT + j), wout[:, :, 256 * j:256 * j + 256], k=8)
            for u in range(6):
                load(ring(MOE0 + u), expert_src(0, 0, u))
            with sp.Fori(0, NE - 1) as e:
                for u in range(6):
                    load(ring(MOE0 + 6 + u), expert_src(0, e + 1, u), i=e)
            wfn = w_fnet[0].rearrange("(k p) n -> p k n", p=128)
            for j in range(4):
                load(ring(WF + j), wfn[:, :, 256 * j:256 * j + 256], k=8)
            overflow_loads(0)
            with sp.Fori(0, NE) as e:
                for u in range(6):
                    load(ring(MOE1 + u), expert_src(1, e, u), i=e)
            overflow_loads(1)

        def hold(pool, signal, value):
            pool.wait_ge(signal, value)
            pool.sem_inc(s_hold, 1)

        def overflow_pool(pool, l):
            O = OV[l]
            cnt = pool.value_load(mxi[0:1, 0:1], min_val=0, max_val=TOK)
            with pool.If(cnt > 128):
                for b in (1, 2):
                    with pool.Fori(0, NE) as e:
                        n0 = NE * (b - 1)
                        hold(pool, O["i"], e + (17 * (b - 1) + 1))
                        pool.indirect_dma_start(
                            out=xg[:], out_offset=None, in_=xs,
                            in_offset=bass.IndirectOffsetOnAxis(ap=gix[:, 0:1], axis=0),
                            bounds_check=SLOTS - 1, oob_is_err=False).then_inc(O["g"], 16)
                        hold(pool, O["y"], e * 2 + (2 * n0 + 2))
                        pool.indirect_dma_start(
                            out=ysl, out_offset=bass.IndirectOffsetOnAxis(ap=gix[:, 0:1], axis=0),
                            in_=yrow[:], in_offset=None, bounds_check=SLOTS - 1, oob_is_err=False).then_inc(O["st"], 16)
                        hold(pool, O["st"], e * 16 + 16 * (n0 + 1))

        @block.gpsimd
        def _(pool):
            n = [0]

            def link(ins):
                n[0] += 1
                ins.then_inc(s_pch, 1)
                pool.wait_ge(s_pch, n[0])

            def root(out, in_, tmp, scale, w, done):
                link(nc.gpsimd.tensor_scalar(tmp, in_, scale, EPS, ALU.mult, ALU.add))
                nc.gpsimd.tensor_tensor(out, tmp, cst[:, C_HALF:C_HALF + w], ALU.pow).then_inc(done, 1)

            nc.gpsimd.memset(zpad[:], 0.0).then_inc(s_zp, 1)

            def load_par(m):
                for cond in range(2):
                    pool.dma_start(par[:, 0:2, cond, :], modd[m, cond, 0:2, :].partition_broadcast(128)).then_inc(s_par, 16)

            def load_gate(m):
                pool.dma_start(par[:, 2, :, :], modd[m, :, 2, :].partition_broadcast(128)).then_inc(s_gate, 16)

            def finish(m):
                l, s = divmod(m, 2)
                if m > 1:
                    pool.wait_ge(s_mdone, 16 * (m - 1))
                gain = (norm1_g, norm2_g)[s][l].rearrange("(x n) -> x n", n=128)
                bias = b_mod[l, 3 * D * s:3 * D * (s + 1)].rearrange("(x n) -> x n", n=128)
                link(nc.gpsimd.memset(mgain[0:48, :], 1.0))
                for i in range(2):
                    pool.wait_ge(s_mxs[i], 96 * m)
                pool.dma_start(mset[0:48, :], modx[m - 1].rearrange("c (x n) -> (c x) n", n=128)).then_inc(s_mset, 16)
                for cond in range(2):
                    pool.dma_start(mbias[24 * cond:24 * cond + 24, :], bias).then_inc(s_mset, 16)
                    pool.dma_start(mgain[24 * cond + 8:24 * cond + 16, :], gain).then_inc(s_mset, 16)
                pool.wait_ge(s_mset, 80 * m)
                link(nc.gpsimd.tensor_tensor(mset[0:48, :], mset[0:48, :], mbias[0:48, :], ALU.add))
                link(nc.gpsimd.tensor_scalar(mset[0:48, :], mset[0:48, :], cst[0:48, C_SC:C_SC + 1], None, ALU.add))
                link(nc.gpsimd.tensor_tensor(mset[0:48, :], mset[0:48, :], mgain[0:48, :], ALU.mult))
                pool.dma_start(modd[m].rearrange("c k (x n) -> (c k x) n", n=128), mset[0:48, :]).then_inc(s_mdone, 16)

            pool.wait_ge(s_mrow, 1)
            for cond in range(2):
                pool.dma_start(modd[0, cond, :, :].unsqueeze(0),
                               modrow[cond:cond + 1, :].rearrange("p (k n) -> p k n", k=3)).then_inc(s_mst, 16)
            pool.wait_ge(s_mst, 32)
            load_par(0)
            load_gate(0)
            for l in range(2):
                pool.wait_ge(s_cst, 16)
                pool.wait_ge(s_sq, 6 * l + 3)
                root(small[:, 3:6], small[:, 0:3], small[:, 6:9], 1.0 / D, 3, s_rstd)
                if l == 0:
                    pool.wait_ge(s_h, 3)
                    pool.dma_start(ck[:], cache_k[0, 0].rearrange("s h e -> s (h e)")).then_inc(s_cach, 16)
                    pool.dma_start(cv[:], cache_v[0, 0].rearrange("s h e -> s (h e)")).then_inc(s_cach, 16)
                    pool.wait_ge(s_qkv, 4)
                    pool.wait_ge(s_z, 4)
                    for t in (1, 2):
                        x = h[:, t, :].rearrange("p (g a w f) -> p g a w f", g=16, a=2, w=2)
                        x1, x2 = x[:, :, :, 0, :], x[:, :, :, 1, :]
                        def tab(o):
                            v = cst[:, o + 32 * (t - 1):o + 32 * t].rearrange("p (a f) -> p a f", a=2)
                            return v.unsqueeze(1).to_broadcast([128, 16, 2, 16])
                        r = [rtmp[:, i, :].rearrange("p (g a f) -> p g a f", g=16, a=2) for i in range(4)]
                        nc.gpsimd.tensor_tensor(r[0], x1, tab(C_COS), ALU.mult)
                        nc.gpsimd.tensor_tensor(r[1], x2, tab(C_SIN), ALU.mult)
                        nc.gpsimd.tensor_tensor(r[2], x1, tab(C_SIN), ALU.mult)
                        link(nc.gpsimd.tensor_tensor(r[3], x2, tab(C_COS), ALU.mult))
                        nc.gpsimd.tensor_tensor(x1, r[0], r[1], ALU.subtract)
                        nc.gpsimd.tensor_tensor(x2, r[2], r[3], ALU.add).then_inc(s_rope, 1)
                        pool.wait_ge(s_rope, t)
                    pool.wait_ge(s_qkv, 6)
                    pool.dma_start(new_k[0, 0].rearrange("s h e -> s (h e)"), h[:, 0, 512:1024]).then_inc(s_kv, 16)
                    pool.dma_start(new_v[0, 0].rearrange("s h e -> s (h e)"), vt[:, 0, :]).then_inc(s_kv, 16)
                    for q in range(PLAIN):
                        pool.wait_ge(s_pev, q + 1)
                        pool.dma_start(modx[q // 12, :, 256 * (q % 12):256 * (q % 12) + 256], mrow2[0:2, q % 2, :]).then_inc(s_mxs[q % 2], 16)
                        if q % 12 == 11:
                            finish(q // 12 + 1)
                    pool.wait_ge(s_o, 12)
                    root(small[:, 24:36], small[:, 12:24], small[:, 36:48], 1.0 / 128, 12, s_rso)
                    pool.wait_ge(s_zv, 3)
                    root(small[:, 57:60], small[:, 48:54].rearrange("p (t s) -> p s t", s=2)[:, 1, :], small[:, 60:63], 1.0, 3, s_rsz)
                if l == 0:
                    pool.wait_ge(s_mdone, 48)
                    pool.wait_ge(s_tp, 6)
                else:
                    pool.wait_ge(s_h, 9)
                load_par(2 * l + 1)
                pool.wait_ge(s_y, 2 * l + 1)
                load_gate(2 * l + 1)
                pool.wait_ge(s_sq, 6 * l + 6)
                root(small[:, 3:6], small[:, 0:3], small[:, 6:9], 1.0 / D, 3, s_rstd)
                pool.wait_ge(s_route, l + 1)
                for t in range(TB):
                    for k in range(2):
                        pool.indirect_dma_start(
                            out=xs, out_offset=bass.IndirectOffsetOnAxis(ap=di[:, 3 * k + t:3 * k + t + 1], axis=0),
                            in_=h[:, t, :], in_offset=None, bounds_check=SLOTS - 1, oob_is_err=False).then_inc(s_xsc, 16)
                nc.gpsimd.memset(xg[:], 0.0).then_inc(s_zp, 1)
                pool.wait_ge(s_zp, l + 2)
                if l == 0:
                    pool.dma_start(yrow[:, 0:8], consts[:, 0:8]).then_inc(s_ysc, 16)

                def gather(k):
                    hold(pool, s_gi, k + 1)
                    pool.indirect_dma_start(
                        out=xg[:], out_offset=None, in_=xs,
                        in_offset=bass.IndirectOffsetOnAxis(ap=gix[:, 0:1], axis=0),
                        bounds_check=SLOTS - 1, oob_is_err=False).then_inc(s_xg, 16)

                pool.wait_ge(s_xsc, 96 * (l + 1))
                gather(18 * l)
                with pool.Fori(0, NE) as e:
                    gather(e + (18 * l + 1))
                    hold(pool, s_yev, e * 2 + (32 * l + 2))
                    pool.indirect_dma_start(
                        out=ysl, out_offset=bass.IndirectOffsetOnAxis(ap=six[:, 0:1], axis=0),
                        in_=yrow[:], in_offset=None, bounds_check=SLOTS - 1, oob_is_err=False).then_inc(s_ysc, 16)
                pool.wait_ge(s_xg, 16 * 17 * (l + 1))
                pool.wait_ge(s_ysc, 16 * (16 * (l + 1) + 1))
                overflow_pool(pool, l)
                if l == 0:
                    load_par(2)
                else:
                    pool.dma_start(par[:, 0, 0, :], final_norm_g.partition_broadcast(128)).then_inc(s_par, 16)
                for t in range(TB):
                    if t or l:
                        pool.wait_ge(s_gu, 3 * l + t)
                    for k, dst in enumerate((ga, gb)):
                        pool.indirect_dma_start(
                            out=dst[:], out_offset=None, in_=ysl,
                            in_offset=bass.IndirectOffsetOnAxis(ap=di[:, 3 * k + t:3 * k + t + 1], axis=0),
                            bounds_check=SLOTS - 1, oob_is_err=False).then_inc(s_ga, 16)
                if l == 0:
                    pool.wait_ge(s_gu, 3)
                    pool.dma_start(dftt[:], dft).then_inc(s_dft, 16)
                    pool.wait_ge(s_y, 2)
                    load_gate(2)
            pool.wait_ge(s_sq, 15)
            root(small[:, 3:6], small[:, 0:3], small[:, 6:9], 1.0 / D, 3, s_rstd)
            pool.wait_ge(s_kv, 32)

        @block.tensor
        def _(pe):
            def mm(out, a, b, start, stop):
                return nc.tensor.matmul(out, a, b, start=start, stop=stop)

            def mm3(out, ah, al, bh, bl, first, last):
                mm(out, ah, bh, first, False)
                mm(out, al, bh, False, False)
                return mm(out, ah, bl, False, last)

            def wait_unit(g, i=None):
                pe.wait_ge(s_lo, g + 1 if i is None else i * 6 + (g + 1))

            def unit(g, k):
                return (H[:, g % SPL, :].rearrange("p (k n) -> p k n", k=k),
                        L[:, g % SPL, :].rearrange("p (k n) -> p k n", k=k))

            def mod():
                with pe.Fori(0, 2) as i:
                    for u in range(6):
                        wait_unit(MOD0 + u, i)
                        wh, wl = unit(MOD0 + u, 8)
                        for k in range(8):
                            last = mm3(ps[0:2, u, 0:256], cH[:, k, :], cL[:, k, :], wh[:, k, :], wl[:, k, :],
                                       k == 0, k == 7)
                        last.then_inc(s_unit, 1)

            def plain(q):
                r = WOUT + q
                pe.wait_ge(s_raw[r % RAW], 16 * (r // RAW + 1))
                if q >= 2:
                    pe.wait_ge(s_pev, q - 1)
                w = raw[:, r % RAW, :].rearrange("p (k n) -> p k n", k=8)
                for k in range(8):
                    last = mm(ps[0:2, 6 + q % 2, 0:256], cS[:, k, :], w[:, k, :], k == 0, k == 7)
                last.then_inc(s_plain, 1)

            def transposes(src, r, ready):
                for t in range(TB):
                    ready(t)
                    v = src[:, t, :].rearrange("p (c k) -> p k c", k=8)
                    for k in range(8):
                        last = nc.tensor.transpose(ps[:, 2 * t + k // 4, 128 * (k % 4):128 * (k % 4) + 128], v[:, k, :], ident)
                    last.then_inc(s_tp, 1)

            def project(g0, n0):
                for j in range(4):
                    wait_unit(g0 + j)
                    if j >= 2:
                        pe.wait_ge(s_yo, n0 + j - 1)
                    wh, wl = unit(g0 + j, 8)
                    for t in range(TB):
                        for k in range(8):
                            c0 = slice(128 * t, 128 * t + 128)
                            last = mm3(ps[:, 4 * (j % 2) + t, 0:256], hTh[:, k, c0], hTl[:, k, c0], wh[:, k, :], wl[:, k, :],
                                       k == 0, k == 7)
                    last.then_inc(s_unit, 1)

            pe.wait_ge(s_cst, 16)
            pe.wait_ge(s_small, 32)
            for i in range(4):
                last = nc.tensor.transpose(ps[:, 7, 32 * i:32 * i + 32], cwr[0:32, 128 * i:128 * i + 128], cst[0:32, 0:32])
            last.then_inc(s_cwt, 1)
            pe.wait_ge(s_cs, 1)
            mod()
            for l in range(2):
                if l == 0:
                    transposes(h, 0, lambda t: pe.wait_ge(s_h, t + 1))
                    pe.wait_ge(s_tl, 6)
                    for j in range(4):
                        wait_unit(WIN + j)
                        if j == 2:
                            pe.wait_ge(s_sig, 1)
                        if j == 3:
                            pe.wait_ge(s_z, 2)
                        wh, wl = unit(WIN + j, 8)
                        for cc in range(2):
                            out = ps[:, 2 * (j % 2) + cc, 0:TOK]
                            for k in range(8):
                                c0 = slice(128 * cc, 128 * cc + 128)
                                last = mm3(out, wh[:, k, c0], wl[:, k, c0], hTh[:, k, :], hTl[:, k, :], k == 0, k == 7)
                        last.then_inc(s_unit, 1)

                    pe.wait_ge(s_z, 4)
                    for j in range(6):
                        g = WIN + 4 + j
                        wait_unit(g)
                        if j >= 2:
                            pe.wait_ge(s_qkv, j - 1)
                        wh, wl = unit(g, 8)
                        for t in range(TB):
                            for k in range(8):
                                c0 = slice(128 * t, 128 * t + 128)
                                last = mm3(ps[:, 4 * (j % 2) + t, 0:256], hTh[:, k, c0], hTl[:, k, c0], wh[:, k, :], wl[:, k, :],
                                           k == 0, k == 7)
                        last.then_inc(s_unit, 1)
                    pe.wait_ge(s_qkv, 6)
                    pe.wait_ge(s_cach, 32)
                    srcs = [h[:, 0, 512:1024], h[:, 0, 0:512], ck[:, :], h[:, 1, 512:1024], h[:, 2, 512:1024],
                            h[:, 1, 0:512], h[:, 2, 0:512]]
                    for j, src in enumerate(srcs):
                        if j == 3:
                            pe.wait_ge(s_rope, 2)
                        for hd in range(4):
                            last = nc.tensor.transpose(ps[:, j, 128 * hd:128 * hd + 128], src[:, 128 * hd:128 * hd + 128], ident)
                        last.then_inc(s_atp, 1)

                    def scores(u):
                        t, hd = divmod(u, 4)
                        if u >= 2:
                            pe.wait_ge(s_p, 2 * (u - 1))
                        k0, nk = (0, 128) if t == 0 else (128, 384)
                        for cc in range(2):
                            pr = slice(64 * cc, 64 * cc + 64)
                            last = mm(ps[:, 2 * (u % 2) + cc, 0:nk], qT[pr, hd, 128 * t:128 * t + 128], kT[pr, hd, k0:k0 + nk],
                                      True, True)
                        last.then_inc(s_sc, 1)

                    def values(u):
                        t, hd = divmod(u, 4)
                        n = 1 if t == 0 else 3
                        p = (pA, pB)[u % 2]
                        pe.wait_ge(s_w, u + 1)
                        if u >= 2:
                            pe.wait_ge(s_o, u - 1)
                        for j in range(n):
                            last = nc.tensor.transpose(ps[:, 4 + u % 2, 128 * j:128 * j + 128], p[:, 0, 128 * j:128 * j + 128], ident)
                        last.then_inc(s_wtp, 1)
                        pe.wait_ge(s_wT, u + 1)
                        hc = slice(128 * hd, 128 * hd + 128)
                        vs = [vt[:, 0, hc]] if t == 0 else [cv[:, hc], vt[:, 1, hc], vt[:, 2, hc]]
                        for j in range(n):
                            last = mm(ps[:, 4 + u % 2, 384:512], wT[:, u % 2, 128 * j:128 * j + 128], vs[j], j == 0, j == n - 1)
                        last.then_inc(s_pv, 1)

                    pe.wait_ge(s_aT, 7)
                    scores(0)
                    for u in range(12):
                        if u + 1 < 12:
                            scores(u + 1)
                        for q in range(PLAIN * u // 12, PLAIN * (u + 1) // 12):
                            plain(q)
                        values(u)
                    pe.wait_ge(s_p, 24)
                    pe.wait_ge(s_conv, 1)
                    for t in range(TB):
                        c0 = 0 if t == 0 else ZS - PAD + 128 * (t - 1)
                        for cc in range(4):
                            last = nc.tensor.transpose(ps[:, t, 128 * cc:128 * cc + 128], conv[:, cc, c0:c0 + 128], ident)
                        last.then_inc(s_ztp, 1)

                    def cat_ready(t):
                        if t == 0:
                            pe.wait_ge(s_zn, 3)
                            pe.wait_ge(s_on, 1)
                            pe.wait_ge(s_o, 12)
                        pe.wait_ge(s_zs, t + 1)
                    transposes(cat, 1, cat_ready)
                    pe.wait_ge(s_tl, 12)
                    project(WOUT, 0)
                else:
                    pe.wait_ge(s_h, 9)
                    pe.wait_ge(s_dft, 16)

                    def stage1(q):
                        if q:
                            pe.wait_ge(s_Pa, 2 * q)
                            pe.wait_ge(s_Pd, 2 * q)
                        for jj in range(2):
                            dc = slice(256 * q + 128 * jj, 256 * q + 128 * jj + 128)
                            mm(ps[:, 2 * jj, 0:256], h[:, 0, dc], dftt[:, 0:256], True, True)
                            mm(ps[:, 2 * jj + 1, :], h[:, 1, dc], dftt[:, 256:768], True, False)
                            last = mm(ps[:, 2 * jj + 1, :], h[:, 2, dc], dftt[:, 768:1280], False, True)
                        last.then_inc(s_s1, 1)

                    def stage2(q):
                        pe.wait_ge(s_Pa, 2 * q + 2)
                        pe.wait_ge(s_Pd, 2 * q + 2)
                        if q >= 2:
                            pe.wait_ge(s_fl, 2 * (q - 1))
                        for oc in range(2):
                            out = ps[:, 4 + 2 * (q % 2) + oc, 0:TOK]
                            for jj in range(2):
                                for s, o in ((0, 1280), (1, 1792)):
                                    w = dftt[:, o + 256 * jj + 128 * oc:o + 256 * jj + 128 * oc + 128]
                                    last = mm(out, w, P[:, q % 2, jj, TOK * s:TOK * s + TOK], jj + s == 0, jj + s == 2)
                        last.then_inc(s_s2, 1)

                    stage1(0)
                    for q in range(4):
                        if q < 3:
                            stage1(q + 1)
                        stage2(q)
                    pe.wait_ge(s_fl, 8)
                    project(WF, 4)
                transposes(h, 2 + l, lambda t: (pe.wait_ge(s_h, 6 * l + 4 + t), pe.wait_ge(s_yo, 4 * l + 4)))
                pe.wait_ge(s_tl, 18 + 6 * l)
                pe.wait_ge(s_wrl, l + 1)
                for t in range(TB):
                    c0 = slice(128 * t, 128 * t + 128)
                    for k in range(8):
                        mm(ps[:, 6, 20 * t:20 * t + 20], hTl[:, k, c0], wrl[:, k, :], k == 0, False)
                        last = mm3(ps[:, 6, 20 * t:20 * t + 20], hTh[:, k, c0], hTl[:, k, c0], wrh[:, k, :], wrl[:, k, :],
                                   False, k == 7)
                last.then_inc(s_lg, 1)
                pe.wait_ge(s_sel, l + 1)
                tri, one = cst[:, C_TRI:C_TRI + 128], cst[:, C_ONE:C_ONE + 128]
                sel = rt[:, 320:368].rearrange("p (t e) -> p t e", t=3)
                for t in range(TB):
                    for b in range(t):
                        mm(ps[:, 7, 16 * t:16 * t + 16], one, sel[:, b, :], b == 0, False)
                    mm(ps[:, 7, 16 * t:16 * t + 16], tri, sel[:, t, :], t == 0, True)
                for b in range(TB):
                    last = mm(ps[:, 7, 48:64], one, sel[:, b, :], b == 0, b == 2)
                last.then_inc(s_cum, 1)

                def x_transposes():
                    v = xg[:].rearrange("p (c k) -> p k c", k=8)
                    for k in range(8):
                        last = nc.tensor.transpose(ps[:, k // 4, 128 * (k % 4):128 * (k % 4) + 128], v[:, k, :], ident)
                    last.then_inc(s_xtp, 1)

                base = MOE0 if l == 0 else MOE1
                pe.wait_ge(s_xg, 16 * (17 * l + 1))
                x_transposes()
                with pe.Fori(0, NE) as e:
                    pe.wait_ge(s_xtl, e * 2 + (34 * l + 2))
                    for u in range(4):
                        wait_unit(base + u, e)
                        wh, wl = unit(base + u, 4)
                        for k in range(4):
                            kk = 4 * (u % 2) + k
                            last = mm3(ps[:, 2 + u // 2, :], hTh[:, kk, 0:128], hTl[:, kk, 0:128], wh[:, k, :], wl[:, k, :],
                                       kk == 0, kk == 7)
                        last.then_inc(s_unit, 1)
                    pe.wait_ge(s_xg, e * 16 + 16 * (17 * l + 2))
                    x_transposes()
                    pe.wait_ge(s_hid, e + (16 * l + 1))
                    v = hid[:].rearrange("p (c k) -> p k c", k=4)
                    for k in range(4):
                        last = nc.tensor.transpose(ps[:, 4, 128 * k:128 * k + 128], v[:, k, :], ident)
                    last.then_inc(s_htp, 1)
                    pe.wait_ge(s_htl, e + (16 * l + 1))
                    for u in range(4, 6):
                        wait_unit(base + u, e)
                        wh, wl = unit(base + u, 2)
                        for k in range(2):
                            kk = 2 * (u - 4) + k
                            for o in range(2):
                                last = mm3(ps[:, 5 + o, :], hTh[:, kk, 128:256], hTl[:, kk, 128:256],
                                           wh[:, k, 512 * o:512 * o + 512], wl[:, k, 512 * o:512 * o + 512], kk == 0, kk == 3)
                        last.then_inc(s_unit, 1)

                O = OV[l]
                pe.wait_ge(s_route, l + 1)
                cnt = pe.value_load(mxi[0:1, 0:1], min_val=0, max_val=TOK)
                with pe.If(cnt > 128):
                    for b in (1, 2):
                        with pe.Fori(0, NE) as e:
                            n0 = NE * (b - 1)
                            pe.wait_ge(O["g"], e * 16 + 16 * (n0 + 1))
                            v = xg[:].rearrange("p (c k) -> p k c", k=8)
                            for k in range(8):
                                last = nc.tensor.transpose(ps[:, k // 4, 128 * (k % 4):128 * (k % 4) + 128], v[:, k, :], ident)
                            last.then_inc(O["tp"], 1)
                            pe.wait_ge(O["xt"], e + (n0 + 1))
                            for u in range(6):
                                if u == 4:
                                    pe.wait_ge(O["hid"], e + (n0 + 1))
                                    v = hid[:].rearrange("p (c k) -> p k c", k=4)
                                    for k in range(4):
                                        last = nc.tensor.transpose(ps[:, 4, 128 * k:128 * k + 128], v[:, k, :], ident)
                                    last.then_inc(O["htp"], 1)
                                    pe.wait_ge(O["ht"], e + (n0 + 1))
                                pe.wait_ge(O["w"][u % 2], e * 48 + 16 * (3 * n0 + u // 2 + 1))
                                if u < 4:
                                    w = wov[:, u % 2, :].rearrange("p (k n) -> p k n", k=4)
                                    for k in range(4):
                                        kk = 4 * (u % 2) + k
                                        last = mm(ps[:, 2 + u // 2, :], xTo[:, kk, :], w[:, k, :], kk == 0, kk == 7)
                                else:
                                    w = wov[:, u % 2, :].rearrange("p (k n) -> p k n", k=2)
                                    for k in range(2):
                                        kk = 2 * (u - 4) + k
                                        for o in range(2):
                                            last = mm(ps[:, 5 + o, :], hTo[:, kk, :], w[:, k, 512 * o:512 * o + 512], kk == 0, kk == 3)
                                last.then_inc(O["u"], 1)

        def overflow_act(act, l):
            O = OV[l]
            act.wait_ge(s_route, l + 1)
            cnt = act.value_load(mxi[0:1, 0:1], min_val=0, max_val=TOK)
            with act.If(cnt > 128):
                for b in (1, 2):
                    with act.Fori(0, NE) as e:
                        n0 = NE * (b - 1)
                        act.wait_ge(O["tp"], e + (n0 + 1))
                        for j in range(2):
                            last = nc.scalar.activation(xTo[:, 4 * j:4 * j + 4, :],
                                                        ps[:, j, :].rearrange("p (k n) -> p k n", k=4), ACT.Copy)
                        last.then_inc(O["xt"], 1)
                        act.wait_ge(O["u"], e * 6 + (6 * n0 + 4))
                        nc.scalar.activation(sg[:], ps[:, 2, :], ACT.Silu).then_inc(O["sg"], 1)
                        act.wait_ge(O["htp"], e + (n0 + 1))
                        nc.scalar.activation(hTo[:], ps[:, 4, :].rearrange("p (k n) -> p k n", k=4), ACT.Copy).then_inc(O["ht"], 1)
                        act.wait_ge(O["u"], e * 6 + (6 * n0 + 6))
                        for o in range(2):
                            nc.scalar.activation(yrow[:, 512 * o:512 * o + 512], ps[:, 5 + o, :], ACT.Copy).then_inc(O["y"], 1)

        @block.scalar
        def _(act):
            def split(g, i=None):
                n = 16 * (ring(g) // RAW + 1)
                act.wait_ge(s_raw[g % RAW], n if i is None else i * 16 + n)
                if g >= SPL:
                    act.wait_ge(s_unit, g - SPL + 1 if i is None else i * 6 + (g - SPL + 1))
                nc.scalar.activation(H[:, g % SPL, :], raw[:, g % RAW, :], ACT.Copy).then_inc(s_hi, 1)

            def squares(j):
                for t in range(TB):
                    nc.scalar.activation(h[:, t, :], y[:, t, :], ACT.Square, accum_out=small[:, t:t + 1]).then_inc(s_sq, 1)

            def t_hi(r):
                for t in range(TB):
                    act.wait_ge(s_tp, 3 * r + t + 1)
                    for b in range(2):
                        nc.scalar.activation(hTh[:, 4 * b:4 * b + 4, 128 * t:128 * t + 128],
                                             ps[:, 2 * t + b, :].rearrange("p (k n) -> p k n", k=4), ACT.Copy).then_inc(s_th, 1)

            def f_hi(q):
                act.wait_ge(s_s2, q + 1)
                for oc in range(2):
                    nc.scalar.activation(hTh[:, 2 * q + oc, :], ps[:, 4 + 2 * (q % 2) + oc, 0:TOK], ACT.Copy).then_inc(s_fh, 1)

            act.dma_start(cT[:, 0, :], c_ctx.rearrange("(p k) -> p k", p=128)).then_inc(s_cT, 16)
            act.dma_start(cT[:, 1, :], c[0].rearrange("(p k) -> p k", p=128)).then_inc(s_cT, 16)
            act.dma_start(cst[:], consts).then_inc(s_cst, 16)
            act.dma_start(bmod[0:2, :], b_mod[0, 0:3 * D].partition_broadcast(2)).then_inc(s_bmod, 16)
            act.dma_start(gn[0:2, :], norm1_g[0].partition_broadcast(2)).then_inc(s_gn, 16)
            act.dma_start(cwr[0:31, :], conv_w[0]).then_inc(s_small, 16)
            act.dma_start(cwr[31:32, :], conv_b[0:1, :]).then_inc(s_small, 16)
            act.dma_start(y[:, 0, :], x_prompt[0]).then_inc(s_yin, 16)
            act.dma_start(y[:, 1:3, :], x_sample[0].rearrange("(t p) n -> p t n", p=128)).then_inc(s_yin, 16)
            for i, v in enumerate((lambda_q1, lambda_k1, lambda_q2, lambda_k2)):
                act.dma_start(lamv[:, i, :], v[0].partition_broadcast(128)).then_inc(s_yin, 16)
            act.dma_start(lnb[:, 0, :], conv_ln_g[0].partition_broadcast(128)).then_inc(s_yin, 16)
            act.dma_start(lnb[:, 1, :], conv_ln_b[0].partition_broadcast(128)).then_inc(s_yin, 16)
            act.dma_start(sub[:], subln_g[0].partition_broadcast(128)).then_inc(s_yin, 16)
            for l in range(2):
                act.dma_start(brt[:, l, 0:4], b_router_group[l].partition_broadcast(128)).then_inc(s_yin, 16)
                act.dma_start(brt[:, l, 4:20], b_router_expert[l].partition_broadcast(128)).then_inc(s_yin, 16)

            def router_in(l):
                act.dma_start(wr[:, :, 0:4], w_router_group[l].rearrange("(p k) n -> p k n", p=128)).then_inc(s_wrin, 16)
                act.dma_start(wr[:, :, 4:20], w_router_expert[l].rearrange("(p k) n -> p k n", p=128)).then_inc(s_wrin, 16)
            router_in(0)
            act.wait_ge(s_cT, 32)
            nc.scalar.activation(cS[:].rearrange("p k c -> p c k"), cT[:], ACT.Silu).then_inc(s_sil, 1)
            act.wait_ge(s_sil, 1)
            nc.scalar.activation(cH[:], cS[:], ACT.Copy).then_inc(s_sil, 1)
            for g in range(SPL):
                split(g)
            with act.Fori(0, 2) as i:
                for u in range(6):
                    split(MOD0 + SPL + u, i)
            act.wait_ge(s_cwt, 1)
            nc.scalar.activation(cw[:].rearrange("p a b -> p (a b)"), ps[:, 7, 0:128], ACT.Copy).then_inc(s_cw, 1)
            act.wait_ge(s_lam, 1)
            nc.scalar.activation(lams[:, 2:4], lams[:, 0:2], ACT.Exp).then_inc(s_le, 1)
            for l in range(2):
                if l == 0:
                    act.wait_ge(s_yin, 16 * 13)
                    act.wait_ge(s_mrow, 1)
                    squares(0)
                    t_hi(0)
                    for j in range(4):
                        if j % 2 == 0:
                            act.wait_ge(s_unit, WIN + j + 1)
                            if j:
                                act.wait_ge(s_z, 2)
                            nc.scalar.activation(sig[:], ps[:, 0:2, 0:TOK], ACT.Sigmoid).then_inc(s_sig, 1)
                        split(WIN + j + SPL)
                    for j in range(6):
                        act.wait_ge(s_unit, WIN + 4 + j + 1)
                        if j < 4:
                            dst = h[:, :, 256 * j:256 * j + 256]
                        else:
                            dst = vt[:, :, 256 * (j - 4):256 * (j - 4) + 256]
                        b = 4 * (j % 2)
                        nc.scalar.activation(dst, ps[:, b:b + 3, 0:256], ACT.Copy).then_inc(s_qkv, 1)
                        if j < 3:
                            split(WIN + 4 + j + SPL)
                    dsts = [kT[:, :, 0:128], qT[:, :, 0:128], kT[:, :, 128:256], kT[:, :, 256:384], kT[:, :, 384:512],
                            qT[:, :, 128:256], qT[:, :, 256:384]]
                    for j, dst in enumerate(dsts):
                        act.wait_ge(s_atp, j + 1)
                        nc.scalar.activation(dst, ps[:, j, :].rearrange("p (k n) -> p k n", k=4), ACT.Copy).then_inc(s_aT, 1)

                    def exps(u):
                        nk = 128 if u < 4 else 384
                        act.wait_ge(s_nm, u + 1)
                        if u >= 2:
                            act.wait_ge(s_wtp, u - 1)
                        for cc in range(2):
                            nc.scalar.activation((pA, pB)[u % 2][:, cc, 0:nk], ps[:, 2 * (u % 2) + cc, 0:nk], ACT.Exp,
                                                 bias=small[:, 64 + 2 * u + cc:65 + 2 * u + cc], scale=0.125,
                                                 accum_out=small[:, 88 + 2 * u + cc:89 + 2 * u + cc]).then_inc(s_p, 1)

                    exps(0)
                    for u in range(12):
                        t, hd = divmod(u, 4)
                        n = 128 if t == 0 else 384
                        if u + 1 < 12:
                            exps(u + 1)
                        for q in range(PLAIN * u // 12, PLAIN * (u + 1) // 12):
                            act.wait_ge(s_plain, q + 1)
                            if q >= 2:
                                act.wait_ge(s_mxs[q % 2], 16 * (q // 2))
                            nc.scalar.activation(mrow2[0:2, q % 2, :], ps[0:2, 6 + q % 2, 0:256], ACT.Copy).then_inc(s_pev, 1)
                        act.wait_ge(s_wtp, u + 1)
                        if u >= 2:
                            act.wait_ge(s_pv, u - 1)
                        nc.scalar.activation(wT[:, u % 2, 0:n], ps[:, 4 + u % 2, 0:n], ACT.Copy).then_inc(s_wT, 1)
                        act.wait_ge(s_pv, u + 1)
                        dst = cat[:, t, 512 + 128 * hd:640 + 128 * hd]
                        nc.scalar.activation(dst, ps[:, 4 + u % 2, 384:512], ACT.Square,
                                             accum_out=small[:, 12 + u:13 + u]).then_inc(s_ach, 1)
                        act.wait_ge(s_ach, u + 1)
                        nc.scalar.activation(dst, ps[:, 4 + u % 2, 384:512], ACT.Copy).then_inc(s_o, 1)
                    for j in range(SPL):
                        split(WOUT + j)
                    for t in range(TB):
                        act.wait_ge(s_zn, t + 1)
                        nc.scalar.activation(cat[:, t, 0:512], cat[:, t, 0:512], ACT.Silu).then_inc(s_zs, 1)
                    t_hi(1)
                    for j in range(4):
                        split(WOUT + j + SPL)
                else:
                    act.wait_ge(s_y, 2)
                    router_in(1)
                    squares(2)
                    for q in range(4):
                        act.wait_ge(s_s1, q + 1)
                        for jj in range(2):
                            nc.scalar.activation(
                                P[:, q % 2, jj, :].rearrange("p (s n) -> p s n", s=2)[:, :, 128:384],
                                ps[:, 2 * jj + 1, :].rearrange("p (s n) -> p s n", s=2), ACT.Copy).then_inc(s_Pa, 1)
                        if q:
                            f_hi(q - 1)
                    f_hi(3)
                    for j in range(4):
                        split(WF + j + SPL)
                act.wait_ge(s_y, 2 * l + 1)
                act.wait_ge(s_kv, 32)
                squares(2 * l + 1)
                act.wait_ge(s_wrin, 32 * (l + 1))
                nc.scalar.activation(wrh[:], wr[:], ACT.Copy).then_inc(s_wrh, 1)
                t_hi(2 + l)
                act.wait_ge(s_rg, l + 1)
                nc.scalar.activation(rt[:, 72:84], rt[:, 60:72], ACT.Exp).then_inc(s_re, 1)
                act.wait_ge(s_rd, l + 1)
                nc.scalar.activation(rt[:, 303:306], rt[:, 300:303], ACT.Exp).then_inc(s_re2, 1)

                def x_hi(v):
                    act.wait_ge(s_xtp, v)
                    for b in range(2):
                        nc.scalar.activation(hTh[:, 4 * b:4 * b + 4, 0:128],
                                             ps[:, b, :].rearrange("p (k n) -> p k n", k=4), ACT.Copy).then_inc(s_xth, 1)

                base = MOE0 if l == 0 else MOE1
                x_hi(v=17 * l + 1)

                def expert(e, more):
                    nc.scalar.activation(small[:, 159:160], cst[:, C_ONE:C_ONE + 1], ACT.Silu).then_inc(s_ach, 1)

                    def sp_(u):
                        if more or u < 3:
                            split(base + u + SPL, e)
                    sp_(0)
                    sp_(1)
                    act.wait_ge(s_unit, e * 6 + (base + 2))
                    nc.scalar.activation(sg[:], ps[:, 2, :], ACT.Silu).then_inc(s_sg, 1)
                    sp_(2)
                    x_hi(v=e + (17 * l + 2))
                    act.wait_ge(s_htp, e + (16 * l + 1))
                    nc.scalar.activation(hTh[:, 0:4, 128:256], ps[:, 4, :].rearrange("p (k n) -> p k n", k=4),
                                         ACT.Copy).then_inc(s_hth, 1)
                    sp_(3)
                    sp_(4)
                    act.wait_ge(s_unit, e * 6 + (base + 6))
                    for o in range(2):
                        nc.scalar.activation(yrow[:, 512 * o:512 * o + 512], ps[:, 5 + o, :], ACT.Copy).then_inc(s_yev, 1)
                    sp_(5)

                if l == 0:
                    with act.Fori(0, NE) as e:
                        expert(e, True)
                else:
                    with act.Fori(0, NE - 1) as e:
                        expert(e, True)
                    expert(NE - 1, False)
                overflow_act(act, l)
            act.wait_ge(s_y, 4)
            squares(4)
            for t in range(TB):
                act.wait_ge(s_h, 12 + t + 1)
                dst = y_prompt[0] if t == 0 else y_sample[0, 128 * (t - 1):128 * t, :]
                act.dma_start(dst, h[:, t, :]).then_inc(s_out, 16)
            act.wait_ge(s_out, 48)

        def route(dve, link, l):
            V = nc.vector

            def b3(x, w):
                return x.unsqueeze(2).to_broadcast([128, 3, w])

            def bc(lo, w):
                return cst[:, lo:lo + w].unsqueeze(1).to_broadcast([128, 3, w])

            def v(lo, w):
                return rt[:, lo:lo + 3 * w].rearrange("p (t w) -> p t w", t=3)

            def first_max(d, consts, w, tmp, mn, out):
                link(V.scalar_tensor_tensor(out=tmp, in0=d, scalar=0.0, in1=bc(consts, w), op0=ALU.is_equal, op1=ALU.mult))
                link(V.tensor_reduce(out=mn, in_=tmp, axis=AX.X, op=ALU.min))
                link(V.tensor_tensor(out, bc(consts, w), b3(mn, w), ALU.is_equal))

            lg, gs, eg, tg, ohg, mg = v(0, 20), v(60, 4), v(72, 4), v(84, 4), v(96, 4), v(108, 4)
            gmax, sumg, gp, mn = rt[:, 120:123], rt[:, 123:126], rt[:, 126:129], rt[:, 129:132]
            ml, d, oh1, sel, oh2, ml2, pos, t16 = (v(132, 16), v(180, 16), v(228, 16), v(320, 16), v(368, 16), v(416, 16),
                                                  v(464, 16), v(512, 16))
            m1, m2 = rt[:, 276:279], rt[:, 279:282]
            dm, r, w1, w2, rp = rt[:, 300:303], rt[:, 303:306], rt[:, 306:309], rt[:, 309:312], rt[:, 312:315]
            df, gt, mx = rt[:, 560:566], rt[:, 640:691], rt[:, 700:701]
            dve.wait_ge(s_lg, l + 1)
            link(V.tensor_tensor(lg, ps[:, 6, 0:60].rearrange("p (t w) -> p t w", t=3),
                                 brt[:, l, :].unsqueeze(1).to_broadcast([128, 3, 20]), ALU.add))
            link(V.tensor_reduce(out=gmax, in_=lg[:, :, 0:4], axis=AX.X, op=ALU.max))
            V.tensor_tensor(gs, lg[:, :, 0:4], b3(gmax, 4), ALU.subtract).then_inc(s_rg, 1)
            dve.wait_ge(s_rg, l + 1)
            first_max(gs, C_J4, 4, tg, mn, ohg)
            link(V.tensor_scalar(mg, ohg, 1e30, -1e30, ALU.mult, ALU.add))
            ml4 = rt[:, 132:180].rearrange("p (t g e) -> p t g e", t=3, g=4)

            def ge(x):
                return x.unsqueeze(3).to_broadcast([128, 3, 4, 4])
            link(V.tensor_tensor(ml4, lg[:, :, 4:20].rearrange("p t (g e) -> p t g e", g=4), ge(ohg), ALU.mult))
            link(V.tensor_tensor(ml4, ml4, ge(mg), ALU.add))
            link(V.tensor_reduce(out=m1, in_=ml, axis=AX.X, op=ALU.max))
            link(V.tensor_tensor(d, ml, b3(m1, 16), ALU.subtract))
            first_max(d, C_J16, 16, t16, mn, oh1)
            link(V.scalar_tensor_tensor(out=ml2, in0=oh1, scalar=-3e30, in1=ml, op0=ALU.mult, op1=ALU.add))
            link(V.tensor_reduce(out=m2, in_=ml2, axis=AX.X, op=ALU.max))
            V.tensor_tensor(dm, m2, m1, ALU.subtract).then_inc(s_rd, 1)
            link(V.tensor_tensor(d, ml2, b3(m2, 16), ALU.subtract))
            first_max(d, C_J16, 16, t16, mn, oh2)
            V.tensor_tensor(sel, oh1, oh2, ALU.add).then_inc(s_sel, 1)
            dve.wait_ge(s_re, l + 1)
            link(V.tensor_reduce(out=sumg, in_=eg, axis=AX.X, op=ALU.add))
            dve.wait_ge(s_re2, l + 1)
            link(V.tensor_scalar(rp, r, 1.0, None, ALU.add))
            link(V.tensor_tensor(rp, rp, sumg, ALU.mult))
            link(V.reciprocal(w1, rp))
            link(V.tensor_tensor(w2, w1, r, ALU.mult))
            dve.wait_ge(s_cum, l + 1)
            link(V.memset(rt[:, 592:640], 0.0))
            sums = [rt[:, 592:616], rt[:, 616:640]]
            link(V.tensor_copy(sums[0][:, 8:24], ps[:, 7, 48:64]))
            for i, k in enumerate((1, 2, 4, 8)):
                a, b = sums[i % 2], sums[1 - i % 2]
                link(V.tensor_tensor(b[:, 8:24], a[:, 8:24], a[:, 8 - k:24 - k], ALU.add))
            off = sums[1][:, 8:24]
            link(V.tensor_tensor(off, sums[0][:, 8:24], ps[:, 7, 48:64], ALU.subtract))
            link(V.tensor_tensor(pos, ps[:, 7, 0:48].rearrange("p (t w) -> p t w", t=3),
                                 off.unsqueeze(1).to_broadcast([128, 3, 16]), ALU.add))
            for k, oh in enumerate((oh1, oh2)):
                link(V.tensor_tensor(t16, pos, oh, ALU.mult))
                link(V.tensor_reduce(out=df[:, 3 * k:3 * k + 3], in_=t16, axis=AX.X, op=ALU.add))
            link(V.tensor_copy(di[:, 0:6], df))
            link(V.memset(gt, 0.0))
            for b in range(3):
                link(V.tensor_scalar(gt[:, 17 * b:17 * b + 16], ps[:, 7, 48:64], cst[:, C_P + b:C_P + b + 1], BIG,
                                     ALU.is_le, ALU.mult))
            gt3 = gt.rearrange("p (b e) -> p b e", b=3)[:, :, 0:16]
            link(V.tensor_tensor(gt3, gt3, off.unsqueeze(1).to_broadcast([128, 3, 16]), ALU.add))
            link(V.tensor_tensor(gtab[:, 0:51], gt, cst[:, C_EP:C_EP + 51], ALU.add))
            link(V.tensor_reduce(out=mx, in_=ps[:, 7, 48:64], axis=AX.X, op=ALU.max))
            V.tensor_copy(mxi[:, 0:1], mx).then_inc(s_route, 1)
            dve.wait_ge(s_route, l + 1)

        @block.vector
        def _(dve):
            n = [0]

            def link(ins):
                n[0] += 1
                ins.then_inc(s_dch, 1)
                dve.wait_ge(s_dch, n[0])

            def rest(g, i=None):
                dve.wait_ge(s_hi, g + 1 if i is None else i * 6 + (g + 1))
                nc.vector.tensor_tensor(L[:, g % SPL, :], raw[:, g % RAW, :], H[:, g % SPL, :].bitcast(f32),
                                        ALU.subtract).then_inc(s_lo, 1)

            def t_lo(r):
                for j in range(6):
                    dve.wait_ge(s_th, 6 * r + j + 1)
                    t, b = divmod(j, 2)
                    hs = (slice(None), slice(4 * b, 4 * b + 4), slice(128 * t, 128 * t + 128))
                    nc.vector.tensor_tensor(hTl[hs], ps[:, j, :].rearrange("p (k n) -> p k n", k=4),
                                            hTh[hs].bitcast(f32), ALU.subtract).then_inc(s_tl, 1)

            def mod():
                dve.wait_ge(s_bmod, 16)
                with dve.Fori(0, 2) as i:
                    for u in range(6):
                        dve.wait_ge(s_unit, i * 6 + (MOD0 + u + 1))
                        col = ds(i * 1536 + 256 * u, 256)
                        nc.vector.tensor_tensor(modrow[0:2, col], ps[0:2, u, 0:256], bmod[0:2, col], ALU.add).then_inc(s_mev, 1)
                        rest(MOD0 + SPL + u, i)
                dve.wait_ge(s_mev, 12)
                dve.wait_ge(s_gn, 16)
                r = modrow[0:2, D:2 * D]
                nc.vector.scalar_tensor_tensor(out=r, in0=r, scalar=1.0, in1=gn[0:2, :], op0=ALU.add, op1=ALU.mult).then_inc(s_mrow, 1)

            def norm(j):
                dve.wait_ge(s_rstd, j + 1)
                dve.wait_ge(s_par, 32 * (j + 1))
                for t in range(TB):
                    cond = min(t, 1)
                    link(nc.vector.scalar_tensor_tensor(out=h[:, t, :], in0=y[:, t, :], scalar=small[:, 3 + t:4 + t],
                                                        in1=par[:, 1, cond, :], op0=ALU.mult, op1=ALU.mult))
                    nc.vector.tensor_tensor(h[:, t, :], h[:, t, :], par[:, 0, cond, :], ALU.add).then_inc(s_h, 1)

            def project(g0):
                dve.wait_ge(s_gate, 16 if g0 == WOUT else 48)
                for j in range(4):
                    dve.wait_ge(s_unit, g0 + j + 1)
                    c0 = slice(256 * j, 256 * j + 256)
                    for t in range(TB):
                        ins = nc.vector.tensor_tensor(tmp3[:, t, :], ps[:, 4 * (j % 2) + t, 0:256], par[:, 2, min(t, 1), c0], ALU.mult)
                        if t < 2:
                            ins.then_inc(s_dch, 1)
                            n[0] += 1
                        else:
                            ins.then_inc(s_yo, 1)
                    dve.wait_ge(s_dch, n[0])
                    dve.wait_ge(s_yo, (0 if g0 == WOUT else 4) + j + 1)
                    link(nc.vector.tensor_tensor(y[:, :, c0], y[:, :, c0], tmp3[:], ALU.add))
                    if j == 3:
                        nc.vector.memset(rt[:, 719:720], 0.0).then_inc(s_y, 1)
                    rest(g0 + j + SPL)

            dve.wait_ge(s_sil, 2)
            nc.vector.tensor_tensor(cL[:], cS[:], cH[:].bitcast(f32), ALU.subtract).then_inc(s_cs, 1)
            for g in range(SPL):
                rest(g)
            dve.wait_ge(s_yin, 16 * 13)
            for i in range(2):
                last = nc.vector.scalar_tensor_tensor(out=rt[:, 64 * i:64 * i + 64], in0=lamv[:, 2 * i, :], scalar=1.0,
                                                      in1=lamv[:, 2 * i + 1, :], op0=ALU.mult, op1=ALU.mult,
                                                      accum_out=lams[:, i:i + 1])
            last.then_inc(s_lam, 1)
            for l in range(2):
                if l == 0:
                    mod()
                    dve.wait_ge(s_le, 1)
                    link(nc.vector.tensor_tensor(lams[:, 4:5], lams[:, 3:4], lams[:, 2:3], ALU.subtract))
                    link(nc.vector.tensor_scalar(lams[:, 5:6], lams[:, 4:5], -0.2, None, ALU.add))
                    norm(0)
                    t_lo(0)
                    dve.wait_ge(s_zp, 1)
                    for j in range(4):
                        if j % 2:
                            i = j // 2
                            dve.wait_ge(s_unit, WIN + j + 1)
                            dve.wait_ge(s_sig, i + 1)
                            for a, b, o in ((0, 128, PAD), (128, 384, ZS)):
                                nc.vector.tensor_tensor(zpad[:, 2 * i:2 * i + 2, o:o + b - a], ps[:, 2:4, a:b], sig[:, :, a:b],
                                                        ALU.mult).then_inc(s_z, 1)
                        rest(WIN + j + SPL)
                    for j in range(3):
                        rest(WIN + 4 + j + SPL)
                    cn = [0]
                    dve.wait_ge(s_cw, 1)
                    dve.wait_ge(s_rope, 2)
                    dve.wait_ge(s_z, 4)

                    def taps(t0, t1):
                        for tap in range(t0, t1):
                            if tap:
                                dve.wait_ge(s_tap, 4 * tap)
                            for cc in range(4):
                                src = zpad[:, cc, tap:tap + CL]
                                if tap == 0:
                                    ins = nc.vector.tensor_scalar(conv[:, cc, :], src, cw[:, cc, 0:1], cw[:, cc, 31:32],
                                                                  ALU.mult, ALU.add)
                                else:
                                    ins = nc.vector.scalar_tensor_tensor(out=conv[:, cc, :], in0=src, scalar=cw[:, cc, tap:tap + 1],
                                                                         in1=conv[:, cc, :], op0=ALU.mult, op1=ALU.add)
                                ins.then_inc(s_tap, 1)

                    def neg_max(u):
                        nk = 128 if u < 4 else 384
                        dve.wait_ge(s_sc, u + 1)
                        b = 2 * (u % 2)
                        link(nc.vector.tensor_reduce(out=small[:, 112 + 2 * u:114 + 2 * u], in_=ps[:, b:b + 2, 0:nk], axis=AX.X,
                                                     op=ALU.max, negate=True))
                        nc.vector.tensor_scalar(small[:, 64 + 2 * u:66 + 2 * u], small[:, 112 + 2 * u:114 + 2 * u], 0.125, None,
                                                ALU.mult).then_inc(s_nm, 1)

                    taps(0, 4)
                    neg_max(0)
                    for u in range(12):
                        nk = 128 if u < 4 else 384
                        if u + 1 < 12:
                            neg_max(u + 1)
                        p = (pA, pB)[u % 2]
                        dve.wait_ge(s_p, 2 * u + 2)
                        rs = small[:, 136 + 2 * u:138 + 2 * u]
                        link(nc.vector.reciprocal(rs, small[:, 88 + 2 * u:90 + 2 * u]))
                        link(nc.vector.tensor_scalar(rs[:, 1:2], rs[:, 1:2], lams[:, 5:6], None, ALU.mult))
                        link(nc.vector.tensor_scalar(p[:, 0, 0:nk], p[:, 0, 0:nk], rs[:, 0:1], None, ALU.mult))
                        nc.vector.scalar_tensor_tensor(out=p[:, 0, 0:nk], in0=p[:, 1, 0:nk], scalar=rs[:, 1:2],
                                                       in1=p[:, 0, 0:nk], op0=ALU.mult, op1=ALU.add).then_inc(s_w, 1)
                        taps(4 + 27 * u // 12, 4 + 27 * (u + 1) // 12)
                    dve.wait_ge(s_tap, 4 * TAPS)
                    nc.vector.memset(rt[:, 718:719], 0.0).then_inc(s_conv, 1)
                    for j in range(SPL):
                        rest(WOUT + j)
                    link(nc.vector.tensor_scalar(sub[:], sub[:], 1.0 - LAM_INIT, None, ALU.mult))
                    dve.wait_ge(s_rso, 1)
                    for u in range(12):
                        t, hd = divmod(u, 4)
                        x = cat[:, t, 512 + 128 * hd:640 + 128 * hd]
                        last = nc.vector.scalar_tensor_tensor(out=x, in0=x, scalar=small[:, 24 + u:25 + u], in1=sub[:],
                                                              op0=ALU.mult, op1=ALU.mult)
                    last.then_inc(s_on, 1)
                    for t in range(TB):
                        dve.wait_ge(s_ztp, t + 1)
                        link(nc.vector.bn_stats(rt[:, 6 * t:6 * t + 6], ps[:, t, :]))
                        nc.vector.bn_aggr(small[:, 48 + 2 * t:50 + 2 * t], rt[:, 6 * t:6 * t + 6]).then_inc(s_zv, 1)
                    dve.wait_ge(s_zv, 3)
                    dve.wait_ge(s_rsz, 1)
                    for t in range(TB):
                        z = cat[:, t, 0:512]
                        link(nc.vector.tensor_scalar(z, ps[:, t, :], small[:, 48 + 2 * t:49 + 2 * t], small[:, 57 + t:58 + t],
                                                     ALU.subtract, ALU.mult))
                        link(nc.vector.tensor_tensor(z, z, lnb[:, 0, :], ALU.mult))
                        nc.vector.tensor_tensor(z, z, lnb[:, 1, :], ALU.add).then_inc(s_zn, 1)
                    t_lo(1)
                    dve.wait_ge(s_kv, 32)
                    project(WOUT)
                else:
                    norm(2)
                    for q in range(4):
                        dve.wait_ge(s_s1, q + 1)
                        for jj in range(2):
                            nc.vector.tensor_copy(
                                P[:, q % 2, jj, :].rearrange("p (s n) -> p s n", s=2)[:, :, 0:128],
                                ps[:, 2 * jj, 0:256].rearrange("p (s n) -> p s n", s=2)).then_inc(s_Pd, 1)
                        for f in ([q - 1] if q else []) + ([3] if q == 3 else []):
                            for oc in range(2):
                                dve.wait_ge(s_fh, 2 * f + oc + 1)
                                nc.vector.tensor_tensor(hTl[:, 2 * f + oc, :], ps[:, 4 + 2 * (f % 2) + oc, 0:TOK],
                                                        hTh[:, 2 * f + oc, :].bitcast(f32), ALU.subtract).then_inc(s_fl, 1)
                    project(WF)
                norm(2 * l + 1)
                dve.wait_ge(s_wrh, l + 1)
                nc.vector.tensor_tensor(wrl[:], wr[:], wrh[:].bitcast(f32), ALU.subtract).then_inc(s_wrl, 1)
                t_lo(2 + l)
                route(dve, link, l)

                base = MOE0 if l == 0 else MOE1

                def x_lo(v):
                    for b in range(2):
                        dve.wait_ge(s_xth, v * 2 + (b - 1))
                        nc.vector.tensor_tensor(hTl[:, 4 * b:4 * b + 4, 0:128], ps[:, b, :].rearrange("p (k n) -> p k n", k=4),
                                                hTh[:, 4 * b:4 * b + 4, 0:128].bitcast(f32), ALU.subtract).then_inc(s_xtl, 1)

                def index(dst, col, done=None):
                    ins = nc.vector.tensor_copy(dst[:, 0:1], gtab[:, ds(col, 1)])
                    if done is not None:
                        ins.then_inc(done, 1)

                def expert(e, more):
                    def rest_(u):
                        if more or u < 3:
                            rest(base + u + SPL, e)
                    for u in range(3):
                        rest_(u)
                    dve.wait_ge(s_sg, e + (16 * l + 1))
                    dve.wait_ge(s_unit, e * 6 + (base + 4))
                    nc.vector.tensor_tensor(hid[:], ps[:, 3, :], sg[:], ALU.mult).then_inc(s_hid, 1)
                    x_lo(e + (17 * l + 2))
                    index(gix, e + 2, s_gi)
                    dve.wait_ge(s_ysc, e * 16 + 16 * (16 * l + 1))
                    index(six, e)
                    dve.wait_ge(s_hth, e + (16 * l + 1))
                    nc.vector.tensor_tensor(hTl[:, 0:4, 128:256], ps[:, 4, :].rearrange("p (k n) -> p k n", k=4),
                                            hTh[:, 0:4, 128:256].bitcast(f32), ALU.subtract).then_inc(s_htl, 1)
                    for u in range(3, 6):
                        rest_(u)

                nc.vector.tensor_copy(gix[:, 0:1], gtab[:, 0:1]).then_inc(s_gi, 1)
                x_lo(17 * l + 1)
                nc.vector.tensor_copy(gix[:, 0:1], gtab[:, 1:2]).then_inc(s_gi, 1)
                if l == 0:
                    with dve.Fori(0, NE) as e:
                        expert(e, True)
                else:
                    with dve.Fori(0, NE - 1) as e:
                        expert(e, True)
                    expert(NE - 1, False)
                O = OV[l]
                cnt = dve.value_load(mxi[0:1, 0:1], min_val=0, max_val=TOK)
                with dve.If(cnt > 128):
                    for b in (1, 2):
                        if b == 1:
                            dve.wait_ge(s_gi, 18 * (l + 1))
                        if b == 2:
                            dve.wait_ge(O["i"], 17)
                        nc.vector.tensor_copy(gix[:, 0:1], gtab[:, 17 * b:17 * b + 1]).then_inc(O["i"], 1)
                        with dve.Fori(0, NE) as e:
                            dve.wait_ge(O["sg"], e + (NE * (b - 1) + 1))
                            nc.vector.tensor_tensor(hid[:], ps[:, 3, :], sg[:], ALU.mult).then_inc(O["hid"], 1)
                            dve.wait_ge(O["st"], e * 16 + 16 * (NE * (b - 1) + 1))
                            index(gix, e + (17 * b + 1), O["i"])
                dve.wait_ge(s_gate, 32 * (l + 1))
                for t in range(TB):
                    dve.wait_ge(s_ga, 32 * (3 * l + t + 1))
                    link(nc.vector.tensor_scalar(ga[:], ga[:], rt[:, 306 + t:307 + t], None, ALU.mult))
                    link(nc.vector.scalar_tensor_tensor(out=gb[:], in0=gb[:], scalar=rt[:, 309 + t:310 + t], in1=ga[:],
                                                        op0=ALU.mult, op1=ALU.add))
                    link(nc.vector.tensor_tensor(gb[:], gb[:], par[:, 2, min(t, 1), :], ALU.mult))
                    nc.vector.tensor_tensor(y[:, t, :], y[:, t, :], gb[:], ALU.add).then_inc(s_gu, 1)
                dve.wait_ge(s_gu, 3 * l + 3)
                nc.vector.memset(rt[:, 719:720], 0.0).then_inc(s_y, 1)
            dve.wait_ge(s_rstd, 5)
            dve.wait_ge(s_par, 144)
            for t in range(TB):
                nc.vector.scalar_tensor_tensor(out=h[:, t, :], in0=y[:, t, :], scalar=small[:, 3 + t:4 + t],
                                               in1=par[:, 0, 0, :], op0=ALU.mult, op1=ALU.mult).then_inc(s_h, 1)



LAM_INIT = 0.8 - 0.6
_INS = ["x_prompt", "x_sample", "cache_k", "cache_v", "c", "c_ctx", "w_mod", "b_mod", "norm1_g", "norm2_g", "w_in_even",
        "conv_w", "conv_b", "conv_ln_g", "conv_ln_b", "lambda_q1", "lambda_k1", "lambda_q2", "lambda_k2", "subln_g",
        "w_out_even", "w_fnet", "w_router_group", "b_router_group", "w_router_expert", "b_router_expert",
        "w_gate_exp", "w_up_exp", "w_down_exp", "final_norm_g"]
_OUTS = [(1, 128, 1024), (1, 256, 1024), (1, 1, 128, 4, 128), (1, 1, 128, 4, 128)]


def kernel(**inputs):
    import numpy as _np
    import concourse.bacc as _bacc
    from concourse import mybir as _mybir
    from concourse.bass_utils import run_bass_kernel_spmd as _run

    nc = _bacc.Bacc("TRN2", target_bir_lowering=False, num_devices=1)
    arrays, args = {}, []
    shaped = {"consts": constants(), "dft": dft_tables()}
    for name in _INS + ["consts", "dft"]:
        a = _np.ascontiguousarray(inputs[name] if name in inputs else shaped[name])
        arrays[f"in_{name}"] = a
        args.append(nc.dram_tensor(f"in_{name}", a.shape, _mybir.dt.from_np(a.dtype), kind="ExternalInput").ap())
    for i, shape in enumerate(_OUTS):
        args.append(nc.dram_tensor(f"out_{i}", shape, _mybir.dt.float32, kind="ExternalOutput").ap())
    build(nc, *args)
    r = _run(nc, [arrays], core_ids=[0])
    return tuple(r.results[0][f"out_{i}"] for i in range(4))
```

```python
import numpy as np
import concourse.bass as bass
from concourse import mybir
from contextlib import ExitStack

D = 1024
TOK = 384
TB = 3
NE = 16
SLOTS = 2 * TOK
F = 512
UNIT = 2048
RAW, SPL = 6, 3
PAD = 15
TAPS = 31
ZS = 2 * PAD + 128
ZL = ZS + 256 + PAD
CL = ZL - 2 * PAD
EPS = 1e-6
BIG = 100000.0

MOD0, WIN, WOUT, MOE0, WF, MOE1, END = 0, 12, 22, 26, 122, 126, 222
PLAIN_N = (18, 9, 9)
PLAIN_AT = (WOUT, MOE0 + PLAIN_N[0], WF + PLAIN_N[0] + PLAIN_N[1])
PLAIN_0 = (0, PLAIN_N[0], PLAIN_N[0] + PLAIN_N[1])


def ring(g):
    return g + sum(n for n, a in zip(PLAIN_N, (WOUT, MOE0, WF)) if g >= a)


def plain_ring(q):
    part = sum(q >= q0 for q0 in PLAIN_0) - 1
    return PLAIN_AT[part] + q - PLAIN_0[part]


C_ID, C_TRI, C_ONE = 0, 128, 256
C_COS, C_SIN = 384, 448
C_J4, C_J16 = 512, 516
C_EP = 548
C_P = 599
C_HALF = 602
C_SC = 618
C_N = 619


def constants():
    c = np.zeros((128, C_N), np.float32)
    p = np.arange(128)
    c[:, C_ID:C_ID + 128] = np.eye(128)
    c[:, C_TRI:C_TRI + 128] = p[:, None] < p[None, :]
    c[:, C_ONE:C_ONE + 128] = 1.0
    inv = (np.float32(10000.0) ** (-np.arange(16, dtype=np.float32) / np.float32(16))).astype(np.float32)
    for b in range(2):
        j = 128 * b + p
        for half, pos in enumerate((j // 64, j % 64)):
            ang = pos.astype(np.float32)[:, None] * inv[None, :]
            o = (2 * b + half) * 16
            c[:, C_COS + o:C_COS + o + 16] = np.cos(ang)
            c[:, C_SIN + o:C_SIN + o + 16] = np.sin(ang)
    c[:, C_J4:C_J4 + 4] = np.arange(4) - 4
    c[:, C_J16:C_J16 + 16] = np.arange(16) - 16
    for b in range(3):
        c[:, C_EP + 17 * b:C_EP + 17 * b + 16] = (128 * b + p)[:, None]
        c[:, C_EP + 17 * b + 16] = BIG
        c[:, C_P + b] = p + 128 * b
    c[:, C_HALF:C_HALF + 16] = -0.5
    c[:, C_SC] = (p < 48) & (p % 24 // 8 == 1)
    return c


def dft_tables():
    t = np.zeros((128, 2304), np.float64)
    p = np.arange(128)

    def ang(rows, n):
        return 2 * np.pi * ((rows[:, None] * np.arange(n)[None, :]) % n) / n

    a = ang(p, 128)
    s = 1 / np.sqrt(128 * 256)
    t[:, 0:128], t[:, 128:256] = np.cos(a) * s, np.sin(a) * s
    s = 1 / np.sqrt(256 * 256)
    for j in range(2):
        a = ang(p + 128 * j, 256)
        t[:, 256 + 512 * j:512 + 512 * j], t[:, 512 + 512 * j:768 + 512 * j] = np.cos(a) * s, np.sin(a) * s
        t[:, 1280 + 256 * j:1536 + 256 * j], t[:, 1792 + 256 * j:2048 + 256 * j] = np.cos(a), -np.sin(a)
    return t.astype(np.float32)


def build(nc, x_prompt, x_sample, cache_k, cache_v, c, c_ctx, w_mod, b_mod, norm1_g, norm2_g, w_in_even,
          conv_w, conv_b, conv_ln_g, conv_ln_b, lambda_q1, lambda_k1, lambda_q2, lambda_k2, subln_g,
          w_out_even, w_fnet, w_router_group, b_router_group, w_router_expert, b_router_expert,
          w_gate_exp, w_up_exp, w_down_exp, final_norm_g, consts, dft,
          y_prompt, y_sample, new_k, new_v):
    f32, f32r, i32 = mybir.dt.float32, mybir.dt.float32r, mybir.dt.int32
    ACT, ALU, AX = mybir.ActivationFunctionType, mybir.AluOpType, mybir.AxisListType
    ds = bass.ds
    ctx = ExitStack()
    with ctx:
        def sem(name):
            return ctx.enter_context(nc.semaphore(name))

        at = [16512]

        def place(name, words, dt=f32, shape=None, over=None):
            off = over if over is not None else at[0]
            if over is None:
                at[0] += -(-4 * words // 32) * 32
            return nc.alloc_sbuf_tensor_at(name, [128] + list(shape or [words]), dt, offset=off)

        raw = place("raw", RAW * UNIT, f32, [RAW, UNIT])
        H = place("H", SPL * UNIT, f32r, [SPL, UNIT])
        L = place("L", SPL * UNIT, f32r, [SPL, UNIT])
        y = place("y", 3 * D, f32, [3, D])
        o_h = at[0]
        h = place("h", 3 * D, f32, [3, D])
        o_th, o_tl = at[0], at[0] + 12 * D
        hTh = place("hTh", 3 * D, f32r, [8, TOK])
        hTl = place("hTl", 3 * D, f32r, [8, TOK])
        modrow = place("modrow", 3 * D, over=o_th)
        kT = place("kT", 2048, f32, [4, 512], over=o_th)
        pA = place("pA", 768, f32, [2, 384], over=o_th + 8192)
        qT = place("qT", 1536, f32, [4, TOK], over=o_tl)
        wT = place("wT", 768, f32, [2, 384], over=o_tl + 6144)
        pB = place("pB", 768, f32, [2, 384], over=o_tl + 9216)
        o_par = at[0]
        par = place("par", 6 * D, f32, [3, 2, D])
        bmod = place("bmod", 3 * D, over=o_par)
        cat = place("cat", 3 * D, f32, [3, D], over=o_par)
        ck = place("ck", 512, over=o_par + 12 * D)
        cv = place("cv", 512, over=o_par + 12 * D + 2048)
        wov = place("wov", 2 * UNIT, f32, [2, UNIT], over=o_par)
        o_s = at[0]
        vt = place("vt", 1536, f32, [3, 512])
        zpad = place("zpad", 4 * ZL, f32, [4, ZL])
        conv = place("conv", 4 * CL, f32, [4, CL])
        sig = place("sig", 768, f32, [2, TOK])
        end_s = at[0]
        rtmp = place("rtmp", 2048, f32, [4, 512], over=o_par)
        tmp3 = place("tmp3", 768, f32, [3, 256], over=o_s)
        gn = place("gn", D, over=o_h)
        xg = place("xg", 1024, over=o_s)
        sg = place("sg", 512, over=o_s + 4096)
        hid = place("hid", 512, over=o_s + 6144)
        yrow = place("yrow", 1024, over=o_s + 8192)
        lgT = place("lgT", TOK, over=o_s + 4096)
        ga = place("ga", 1024, over=o_s + 12288)
        gb = place("gb", 1024, over=o_s + 16384)
        pairs = [(ga, gb), (xg, yrow), (place("ga2", 1024, over=o_th), place("gb2", 1024, over=o_th + 4096))]
        xTo = place("xTo", 1024, f32, [8, 128], over=o_s + 12288)
        hTo = place("hTo", 512, f32, [4, 128], over=o_s + 16384)
        P = place("P", 3072, f32, [2, 2, 768], over=o_s)
        dftt = place("dftt", 2304, over=o_s + 12288)
        mrow_p = [place("mrow_r", 256 * PLAIN_N[1], over=o_s + 12288), place("mrow_c", 256 * PLAIN_N[2], over=o_tl)]
        assert o_s + 12288 + 9216 <= end_s
        cst = place("cst", C_N)
        cT = place("cT", 16, f32, [2, 8])
        cS = place("cS", 16, f32, [8, 2])
        cH = place("cH", 16, f32r, [8, 2])
        cL = place("cL", 16, f32r, [8, 2])
        o_cwr = at[0]
        cwr = place("cwr", 512)
        mrow2 = place("mrow2", 512, f32, [2, 256], over=o_cwr)
        cw = place("cw", 128, f32, [4, 32])
        lnb = place("lnb", 1024, f32, [2, 512])
        o_lamv = at[0]
        lamv = place("lamv", 256, f32, [4, 64])
        mbias = place("mbias", 128, over=o_lamv)
        mgain = place("mgain", 128, over=o_lamv + 512)
        mset = place("mset", 128)
        lams = place("lams", 8)
        sub = place("sub", 128)
        wr = place("wr", 160, f32, [8, 20])
        wrh = place("wrh", 160, f32r, [8, 20])
        wrl = place("wrl", 160, f32r, [8, 20])
        brt = place("brt", 40, f32, [2, 20])
        small = place("small", 160)
        rt = place("rt", 720)
        di = place("di", 8, i32)
        gtab = place("gtab", 52, i32)
        gix = place("gix", 8, i32)
        six = place("six", 8, i32)
        mxi = place("mxi", 8, i32)
        assert at[0] <= 229344, at[0]
        ps = ctx.enter_context(nc.psum_tensor("ps", [128, 8, 512], f32))
        ident = cst[:, C_ID:C_ID + 128]

        modd = nc.dram_tensor("modd", [4, 2, 3, D], f32).ap()
        modx = nc.dram_tensor("modx", [3, 2, 3 * D], f32).ap()
        xs = nc.dram_tensor("xs", [SLOTS, D], f32).ap()
        ysl = nc.dram_tensor("ysl", [SLOTS, D], f32).ap()

        s_raw = [sem(f"raw_loaded{i}") for i in range(RAW)]
        s_hi, s_lo, s_unit = sem("unit_rounded"), sem("unit_split"), sem("unit_used")
        s_cst, s_small, s_yin, s_cT = sem("consts_in"), sem("small_in"), sem("y_in"), sem("cond_in")
        s_bmod, s_gn = sem("bmod_in"), sem("gains_in")
        s_sil, s_cs = sem("cond_silu"), sem("cond_split")
        s_mev, s_mrow, s_mst, s_par = sem("mod_evac"), sem("mod_row"), sem("mod_stored"), sem("par_in")
        s_gate, s_plain, s_pev = sem("gates_in"), sem("plain_used"), sem("plain_evac")
        s_mx2, s_mx3 = sem("products2_stored"), [sem(f"products3_stored{i}") for i in range(2)]
        s_mxs, s_mset, s_mdone = [sem(f"products_stored{i}") for i in range(2)], sem("set_in"), sem("set_done")
        s_sq, s_rstd, s_h = sem("sq_sum"), sem("rstd"), sem("h_ready")
        s_tp, s_th, s_tl = sem("transposed"), sem("t_hi"), sem("t_lo")
        s_sig, s_z, s_qkv = sem("sigmoid"), sem("glu"), sem("qkv_out")
        s_zp, s_rope = sem("pads_zero"), sem("rope")
        s_cwt, s_cw = sem("taps_transposed"), sem("taps_ready")
        s_cach, s_kv = sem("cache_in"), sem("kv_stored")
        s_atp, s_aT, s_sc, s_nm, s_p = sem("qk_transposed"), sem("qk_T"), sem("scores"), sem("neg_max"), sem("probs")
        s_w, s_wtp, s_wT, s_pv, s_o = sem("weights"), sem("w_transposed"), sem("w_T"), sem("pv"), sem("o_out")
        s_lam, s_le, s_rso, s_on = sem("lam_dots"), sem("lam_exp"), sem("o_rstd"), sem("o_normed")
        s_tap = sem("taps_added")
        s_conv, s_ztp, s_zv, s_rsz, s_zn, s_zs = (sem("conv_done"), sem("z_transposed"), sem("z_var"), sem("z_rstd"),
                                                 sem("z_normed"), sem("z_silu"))
        s_yo, s_y = sem("proj_added"), sem("y_ready")
        s_wrin, s_wrh, s_wrl, s_lg = sem("router_in"), sem("router_hi"), sem("router_lo"), sem("logits")
        s_lgT, s_lgc = sem("logits_T"), sem("logits_T_copied")
        s_mx = sem("largest_count")
        s_rg, s_re, s_sel, s_cum, s_route = sem("gate_in"), sem("gate_exp"), sem("selected"), sem("counted"), sem("routed")
        s_xsc, s_gi, s_xg, s_xtp, s_xth, s_xtl = (sem("x_scattered"), sem("idx_ready"), sem("x_gathered"),
                                                 sem("x_transposed"), sem("x_hi"), sem("x_lo"))
        s_sg, s_hid, s_htp, s_hth, s_htl = sem("silu_gate"), sem("hidden"), sem("hid_transposed"), sem("hid_hi"), sem("hid_lo")
        s_yev, s_ysc = sem("y_evac"), sem("y_scattered")
        s_rd, s_re2 = sem("top2_diff"), sem("top2_exp")
        s_ga, s_gu = [sem(f"pair_gathered{t}") for t in range(TB)], sem("pair_used")
        s_dft, s_s1, s_Pa, s_Pd, s_s2 = sem("dft_in"), sem("dft_stage1"), sem("P_act"), sem("P_dve"), sem("dft_stage2")
        s_fh, s_fl = sem("f_hi"), sem("f_lo")
        s_out, s_hold = sem("out_stored"), sem("pool_held")
        s_dch, s_pch, s_ach = sem("dve_chain"), sem("pool_chain"), sem("act_chain")
        OV = [{n: sem(f"ov{l}_{n}") for n in ("g", "i", "u", "tp", "xt", "sg", "hid", "htp", "ht", "y", "st")}
              for l in range(2)]
        for l in range(2):
            OV[l]["w"] = [sem(f"ov{l}_w{i}") for i in range(2)]

        wexp = [t.rearrange("l e (p k) n -> l e p (k n)", p=128) for t in (w_gate_exp, w_up_exp, w_down_exp)]

        def expert_src(l, e, u):
            return wexp[u // 2][l, ds(e, 1), :, (u % 2) * UNIT:(u % 2 + 1) * UNIT].rearrange("a p n -> p (a n)")

        block = ctx.enter_context(nc.Block())

        @block.sync
        def _(sp):
            def freed(r):
                for n, a, q0 in zip(PLAIN_N, PLAIN_AT, PLAIN_0):
                    if a <= r < a + n:
                        return s_plain, q0 + r - a + 1
                return s_lo, r - sum(n for n, a in zip(PLAIN_N, PLAIN_AT) if a < r) + 1

            def load(r, src, k=None, i=None):
                if r >= RAW:
                    done, n = freed(r - RAW)
                    sp.wait_ge(done, n if i is None else i * 6 + n)
                dst = raw[:, r % RAW, :]
                sp.dma_start(dst.rearrange("p (k n) -> p k n", k=k) if k else dst, src).then_inc(s_raw[r % RAW], 16)

            def mod_src(l, col):
                return w_mod[l].rearrange("(p k) n -> p k n", p=128)[:, :, col]

            def overflow_loads(l):
                O = OV[l]
                sp.wait_ge(s_mx, l + 1)
                cnt = sp.value_load(mxi[0:1, 0:1], min_val=0, max_val=TOK)
                with sp.If(cnt > 128):
                    for b in (1, 2):
                        with sp.Fori(0, NE) as e:
                            for u in range(6):
                                n0 = 6 * NE * (b - 1)
                                if u == 0:
                                    sp.wait_ge(O["i"], e + (17 * (b - 1) + 1))
                                if u >= 2:
                                    sp.wait_ge(O["u"], e * 6 + (n0 + u - 1))
                                sp.dma_start(wov[:, u % 2, :], expert_src(l, e, u)).then_inc(O["w"][u % 2], 16)

            for u in range(12):
                load(u, mod_src(0, slice(256 * u, 256 * u + 256)), k=8)
            win = w_in_even[0].rearrange("(p k) n -> p k n", p=128)
            for j, col in enumerate((2, 0, 3, 1, 4, 5, 6, 7, 8, 9)):
                if j == 4:
                    sp.wait_ge(s_par, 32)
                load(WIN + j, win[:, :, 256 * col:256 * col + 256], k=8)
            def mod_loads(q0, q1):
                for q in range(q0, q1):
                    m = q // 12 + 1
                    c0 = 3 * D * (m % 2) + 256 * (q % 12)
                    load(plain_ring(q), mod_src(m // 2, slice(c0, c0 + 256)), k=8)

            mod_loads(0, 18)
            wout = w_out_even[0].rearrange("(p k) n -> p k n", p=128)
            for j in range(4):
                load(ring(WOUT + j), wout[:, :, 256 * j:256 * j + 256], k=8)
            mod_loads(18, 27)
            for l, base in enumerate((MOE0, MOE1)):
                for u in range(6):
                    load(ring(base + u), expert_src(l, 0, u))
                with sp.Fori(0, NE - 1) as e:
                    for u in range(6):
                        load(ring(base + 6 + u), expert_src(l, e + 1, u), i=e)
                if l == 0:
                    mod_loads(27, 33)
                overflow_loads(l)
                if l == 0:
                    mod_loads(33, 36)
                    wfn = w_fnet[0].rearrange("(k p) n -> p k n", p=128)
                    for j in range(4):
                        load(ring(WF + j), wfn[:, :, 256 * j:256 * j + 256], k=8)

        def hold(pool, signal, value):
            pool.wait_ge(signal, value)
            pool.sem_inc(s_hold, 1)

        def overflow_pool(pool, l):
            O = OV[l]
            pool.wait_ge(s_mx, l + 1)
            cnt = pool.value_load(mxi[0:1, 0:1], min_val=0, max_val=TOK)
            with pool.If(cnt > 128):
                for b in (1, 2):
                    with pool.Fori(0, NE) as e:
                        n0 = NE * (b - 1)
                        hold(pool, O["i"], e + (17 * (b - 1) + 1))
                        pool.indirect_dma_start(
                            out=xg[:], out_offset=None, in_=xs,
                            in_offset=bass.IndirectOffsetOnAxis(ap=gix[:, 0:1], axis=0),
                            bounds_check=SLOTS - 1, oob_is_err=False).then_inc(O["g"], 16)
                        hold(pool, O["y"], e * 2 + (2 * n0 + 2))
                        pool.indirect_dma_start(
                            out=ysl, out_offset=bass.IndirectOffsetOnAxis(ap=gix[:, 0:1], axis=0),
                            in_=yrow[:], in_offset=None, bounds_check=SLOTS - 1, oob_is_err=False).then_inc(O["st"], 16)
                        hold(pool, O["st"], e * 16 + 16 * (n0 + 1))

        @block.gpsimd
        def _(pool):
            n = [0]

            def link(ins):
                n[0] += 1
                ins.then_inc(s_pch, 1)
                pool.wait_ge(s_pch, n[0])

            def root(out, in_, tmp, scale, w, done):
                link(nc.gpsimd.tensor_scalar(tmp, in_, scale, EPS, ALU.mult, ALU.add))
                nc.gpsimd.tensor_tensor(out, tmp, cst[:, C_HALF:C_HALF + w], ALU.pow).then_inc(done, 1)

            pool.dma_start(bmod[0:2, :], b_mod[0, 0:3 * D].partition_broadcast(2)).then_inc(s_bmod, 16)
            pool.dma_start(gn[0:2, :], norm1_g[0].partition_broadcast(2)).then_inc(s_gn, 16)
            pool.dma_start(cwr[0:31, :], conv_w[0]).then_inc(s_small, 16)
            pool.dma_start(cwr[31:32, :], conv_b[0:1, :]).then_inc(s_small, 16)
            pool.dma_start(y[:, 0, :], x_prompt[0]).then_inc(s_yin, 16)
            pool.dma_start(y[:, 1:3, :], x_sample[0].rearrange("(t p) n -> p t n", p=128)).then_inc(s_yin, 16)
            for i, v in enumerate((lambda_q1, lambda_k1, lambda_q2, lambda_k2)):
                pool.dma_start(lamv[:, i, :], v[0].partition_broadcast(128)).then_inc(s_yin, 16)
            pool.dma_start(lnb[:, 0, :], conv_ln_g[0].partition_broadcast(128)).then_inc(s_yin, 16)
            pool.dma_start(lnb[:, 1, :], conv_ln_b[0].partition_broadcast(128)).then_inc(s_yin, 16)
            pool.dma_start(sub[:], subln_g[0].partition_broadcast(128)).then_inc(s_yin, 16)
            for l in range(2):
                pool.dma_start(brt[:, l, 0:4], b_router_group[l].partition_broadcast(128)).then_inc(s_yin, 16)
                pool.dma_start(brt[:, l, 4:20], b_router_expert[l].partition_broadcast(128)).then_inc(s_yin, 16)
            nc.gpsimd.memset(zpad[:], 0.0).then_inc(s_zp, 1)

            def load_par(m):
                for cond in range(2):
                    pool.dma_start(par[:, 0:2, cond, :], modd[m, cond, 0:2, :].partition_broadcast(128)).then_inc(s_par, 16)

            def load_gate(m):
                pool.dma_start(par[:, 2, :, :], modd[m, :, 2, :].partition_broadcast(128)).then_inc(s_gate, 16)

            def finish(m):
                l, s = divmod(m, 2)
                if m > 1:
                    pool.wait_ge(s_mdone, 16 * (m - 1))
                gain = (norm1_g, norm2_g)[s][l].rearrange("(x n) -> x n", n=128)
                bias = b_mod[l, 3 * D * s:3 * D * (s + 1)].rearrange("(x n) -> x n", n=128)
                link(nc.gpsimd.memset(mgain[0:48, :], 1.0))
                for i in range(2):
                    if m < 3:
                        pool.wait_ge(s_mxs[i], 96 if m == 1 else 144)
                    else:
                        pool.wait_ge(s_mx3[i], 16)
                if m == 2:
                    pool.wait_ge(s_mx2, 16)
                pool.dma_start(mset[0:48, :], modx[m - 1].rearrange("c (x n) -> (c x) n", n=128)).then_inc(s_mset, 16)
                for cond in range(2):
                    pool.dma_start(mbias[24 * cond:24 * cond + 24, :], bias).then_inc(s_mset, 16)
                    pool.dma_start(mgain[24 * cond + 8:24 * cond + 16, :], gain).then_inc(s_mset, 16)
                pool.wait_ge(s_mset, 80 * m)
                link(nc.gpsimd.tensor_tensor(mset[0:48, :], mset[0:48, :], mbias[0:48, :], ALU.add))
                link(nc.gpsimd.tensor_scalar(mset[0:48, :], mset[0:48, :], cst[0:48, C_SC:C_SC + 1], None, ALU.add))
                link(nc.gpsimd.tensor_tensor(mset[0:48, :], mset[0:48, :], mgain[0:48, :], ALU.mult))
                pool.dma_start(modd[m].rearrange("c k (x n) -> (c k x) n", n=128), mset[0:48, :]).then_inc(s_mdone, 16)

            pool.wait_ge(s_mrow, 1)
            for cond in range(2):
                pool.dma_start(modd[0, cond, :, :].unsqueeze(0),
                               modrow[cond:cond + 1, :].rearrange("p (k n) -> p k n", k=3)).then_inc(s_mst, 16)
            pool.wait_ge(s_mst, 32)
            load_par(0)
            load_gate(0)
            for l in range(2):
                pool.wait_ge(s_cst, 16)
                pool.wait_ge(s_sq, 6 * l + 3)
                root(small[:, 3:6], small[:, 0:3], small[:, 6:9], 1.0 / D, 3, s_rstd)
                if l == 0:
                    pool.wait_ge(s_h, 3)
                    pool.dma_start(ck[:], cache_k[0, 0].rearrange("s h e -> s (h e)")).then_inc(s_cach, 16)
                    pool.dma_start(cv[:], cache_v[0, 0].rearrange("s h e -> s (h e)")).then_inc(s_cach, 16)
                    pool.wait_ge(s_qkv, 4)
                    for t in (1, 2):
                        x = h[:, t, :].rearrange("p (g a w f) -> p g a w f", g=16, a=2, w=2)
                        x1, x2 = x[:, :, :, 0, :], x[:, :, :, 1, :]
                        def tab(o):
                            v = cst[:, o + 32 * (t - 1):o + 32 * t].rearrange("p (a f) -> p a f", a=2)
                            return v.unsqueeze(1).to_broadcast([128, 16, 2, 16])
                        r = [rtmp[:, i, :].rearrange("p (g a f) -> p g a f", g=16, a=2) for i in range(4)]
                        nc.gpsimd.tensor_tensor(r[0], x1, tab(C_COS), ALU.mult)
                        nc.gpsimd.tensor_tensor(r[1], x2, tab(C_SIN), ALU.mult)
                        nc.gpsimd.tensor_tensor(r[2], x1, tab(C_SIN), ALU.mult)
                        link(nc.gpsimd.tensor_tensor(r[3], x2, tab(C_COS), ALU.mult))
                        nc.gpsimd.tensor_tensor(x1, r[0], r[1], ALU.subtract)
                        nc.gpsimd.tensor_tensor(x2, r[2], r[3], ALU.add).then_inc(s_rope, 1)
                        pool.wait_ge(s_rope, t)
                    pool.wait_ge(s_qkv, 6)
                    pool.dma_start(new_k[0, 0].rearrange("s h e -> s (h e)"), h[:, 0, 512:1024]).then_inc(s_kv, 16)
                    pool.dma_start(new_v[0, 0].rearrange("s h e -> s (h e)"), vt[:, 0, :]).then_inc(s_kv, 16)
                    pool.wait_ge(s_o, 12)
                    root(small[:, 24:36], small[:, 12:24], small[:, 36:48], 1.0 / 128, 12, s_rso)
                    pool.wait_ge(s_zv, 3)
                    root(small[:, 57:60], small[:, 48:54].rearrange("p (t s) -> p s t", s=2)[:, 1, :], small[:, 60:63], 1.0, 3, s_rsz)
                finish(2 * l + 1)
                pool.wait_ge(s_mdone, 32 * l + 16)
                if l == 0:
                    pool.wait_ge(s_tp, 6)
                else:
                    pool.wait_ge(s_h, 9)
                load_par(2 * l + 1)
                pool.wait_ge(s_y, 2 * l + 1)
                load_gate(2 * l + 1)
                pool.wait_ge(s_sq, 6 * l + 6)
                root(small[:, 3:6], small[:, 0:3], small[:, 6:9], 1.0 / D, 3, s_rstd)
                nc.gpsimd.memset(xg[:], 0.0).then_inc(s_zp, 1)
                pool.wait_ge(s_route, l + 1)
                for t in range(TB):
                    for k in range(2):
                        pool.indirect_dma_start(
                            out=xs, out_offset=bass.IndirectOffsetOnAxis(ap=di[:, 3 * k + t:3 * k + t + 1], axis=0),
                            in_=h[:, t, :], in_offset=None, bounds_check=SLOTS - 1, oob_is_err=False).then_inc(s_xsc, 16)
                if l == 0:
                    pool.dma_start(yrow[:, 0:8], consts[:, 0:8]).then_inc(s_ysc, 16)

                def gather(k):
                    hold(pool, s_gi, k + 1)
                    pool.indirect_dma_start(
                        out=xg[:], out_offset=None, in_=xs,
                        in_offset=bass.IndirectOffsetOnAxis(ap=gix[:, 0:1], axis=0),
                        bounds_check=SLOTS - 1, oob_is_err=False).then_inc(s_xg, 16)

                pool.wait_ge(s_zp, l + 2)
                pool.wait_ge(s_xsc, 96 * (l + 1))
                gather(18 * l)

                def rows_of(e, between=None):
                    gather(e + (18 * l + 1))
                    if between is not None:
                        finish(between)
                    hold(pool, s_yev, e * 2 + (32 * l + 2))
                    pool.indirect_dma_start(
                        out=ysl, out_offset=bass.IndirectOffsetOnAxis(ap=six[:, 0:1], axis=0),
                        in_=yrow[:], in_offset=None, bounds_check=SLOTS - 1, oob_is_err=False).then_inc(s_ysc, 16)

                with pool.Fori(0, NE - 1) as e:
                    rows_of(e)
                rows_of(NE - 1, between=2 if l == 0 else None)
                pool.wait_ge(s_xg, 16 * 17 * (l + 1))
                pool.wait_ge(s_ysc, 16 * (16 * (l + 1) + 1))
                overflow_pool(pool, l)
                pool.wait_ge(s_mx3[0], 16)
                for t in range(TB):
                    for k, dst in enumerate(pairs[t]):
                        pool.indirect_dma_start(
                            out=dst[:], out_offset=None, in_=ysl,
                            in_offset=bass.IndirectOffsetOnAxis(ap=di[:, 3 * k + t:3 * k + t + 1], axis=0),
                            bounds_check=SLOTS - 1, oob_is_err=False).then_inc(s_ga[t], 16)
                if l == 0:
                    pool.wait_ge(s_mdone, 32)
                    load_par(2)
                else:
                    pool.dma_start(par[:, 0, 0, :], final_norm_g.partition_broadcast(128)).then_inc(s_par, 16)
                if l == 0:
                    pool.wait_ge(s_gu, 1)
                    pool.dma_start(dftt[:], dft).then_inc(s_dft, 16)
                    pool.wait_ge(s_y, 2)
                    load_gate(2)
            for t in range(TB):
                pool.wait_ge(s_sq, 12 + t + 1)
                root(small[:, 3 + t:4 + t], small[:, t:t + 1], small[:, 6 + t:7 + t], 1.0 / D, 1, s_rstd)
            pool.wait_ge(s_kv, 32)

        @block.tensor
        def _(pe):
            def mm(out, a, b, start, stop):
                return nc.tensor.matmul(out, a, b, start=start, stop=stop)

            def mm3(out, ah, al, bh, bl, first, last):
                mm(out, ah, bh, first, False)
                mm(out, al, bh, False, False)
                return mm(out, ah, bl, False, last)

            def wait_unit(g, i=None):
                pe.wait_ge(s_lo, g + 1 if i is None else i * 6 + (g + 1))

            def unit(g, k):
                return (H[:, g % SPL, :].rearrange("p (k n) -> p k n", k=k),
                        L[:, g % SPL, :].rearrange("p (k n) -> p k n", k=k))

            def mod():
                with pe.Fori(0, 2) as i:
                    for u in range(6):
                        wait_unit(MOD0 + u, i)
                        wh, wl = unit(MOD0 + u, 8)
                        for k in range(8):
                            last = mm3(ps[0:2, u, 0:256], cH[:, k, :], cL[:, k, :], wh[:, k, :], wl[:, k, :],
                                       k == 0, k == 7)
                        last.then_inc(s_unit, 1)

            def plain(q, banks):
                r = plain_ring(q)
                pe.wait_ge(s_raw[r % RAW], 16 * (r // RAW + 1))
                if q >= 2:
                    pe.wait_ge(s_pev, q - 1)
                w = raw[:, r % RAW, :].rearrange("p (k n) -> p k n", k=8)
                for k in range(8):
                    last = mm(ps[0:2, banks[q % 2], 0:256], cS[:, k, :], w[:, k, :], k == 0, k == 7)
                last.then_inc(s_plain, 1)

            def transposes(src, r, ready):
                for t in range(TB):
                    ready(t)
                    v = src[:, t, :].rearrange("p (c k) -> p k c", k=8)
                    for k in range(8):
                        last = nc.tensor.transpose(ps[:, 2 * t + k // 4, 128 * (k % 4):128 * (k % 4) + 128], v[:, k, :], ident)
                    last.then_inc(s_tp, 1)

            def project(g0, n0):
                for j in range(4):
                    wait_unit(g0 + j)
                    if j >= 2:
                        pe.wait_ge(s_yo, n0 + j - 1)
                    wh, wl = unit(g0 + j, 8)
                    for t in range(TB):
                        for k in range(8):
                            c0 = slice(128 * t, 128 * t + 128)
                            last = mm3(ps[:, 4 * (j % 2) + t, 0:256], hTh[:, k, c0], hTl[:, k, c0], wh[:, k, :], wl[:, k, :],
                                       k == 0, k == 7)
                    last.then_inc(s_unit, 1)

            pe.wait_ge(s_cs, 1)
            mod()
            pe.wait_ge(s_cst, 16)
            pe.wait_ge(s_small, 32)
            for i in range(4):
                last = nc.tensor.transpose(ps[:, 7, 32 * i:32 * i + 32], cwr[0:32, 128 * i:128 * i + 128], cst[0:32, 0:32])
            last.then_inc(s_cwt, 1)
            for l in range(2):
                if l == 0:
                    transposes(h, 0, lambda t: pe.wait_ge(s_h, t + 1))
                    pe.wait_ge(s_tl, 6)
                    for j in range(4):
                        wait_unit(WIN + j)
                        if j == 2:
                            pe.wait_ge(s_sig, 1)
                        if j == 3:
                            pe.wait_ge(s_z, 2)
                        wh, wl = unit(WIN + j, 8)
                        for cc in range(2):
                            out = ps[:, 2 * (j % 2) + cc, 0:TOK]
                            for k in range(8):
                                c0 = slice(128 * cc, 128 * cc + 128)
                                last = mm3(out, wh[:, k, c0], wl[:, k, c0], hTh[:, k, :], hTl[:, k, :], k == 0, k == 7)
                        last.then_inc(s_unit, 1)

                    pe.wait_ge(s_z, 4)
                    for j in range(6):
                        g = WIN + 4 + j
                        wait_unit(g)
                        if j >= 2:
                            pe.wait_ge(s_qkv, j - 1)
                        wh, wl = unit(g, 8)
                        for t in range(TB):
                            for k in range(8):
                                c0 = slice(128 * t, 128 * t + 128)
                                last = mm3(ps[:, 4 * (j % 2) + t, 0:256], hTh[:, k, c0], hTl[:, k, c0], wh[:, k, :], wl[:, k, :],
                                           k == 0, k == 7)
                        last.then_inc(s_unit, 1)
                    pe.wait_ge(s_qkv, 6)
                    pe.wait_ge(s_cach, 32)
                    srcs = [h[:, 0, 512:1024], h[:, 0, 0:512], ck[:, :], h[:, 1, 512:1024], h[:, 2, 512:1024],
                            h[:, 1, 0:512], h[:, 2, 0:512]]
                    for j, src in enumerate(srcs):
                        if j == 3:
                            pe.wait_ge(s_rope, 2)
                        for hd in range(4):
                            last = nc.tensor.transpose(ps[:, j, 128 * hd:128 * hd + 128], src[:, 128 * hd:128 * hd + 128], ident)
                        last.then_inc(s_atp, 1)

                    def scores(u):
                        t, hd = divmod(u, 4)
                        if u >= 2:
                            pe.wait_ge(s_p, 2 * (u - 1))
                        k0, nk = (0, 128) if t == 0 else (128, 384)
                        for cc in range(2):
                            pr = slice(64 * cc, 64 * cc + 64)
                            last = mm(ps[:, 2 * (u % 2) + cc, 0:nk], qT[pr, hd, 128 * t:128 * t + 128], kT[pr, hd, k0:k0 + nk],
                                      True, True)
                        last.then_inc(s_sc, 1)

                    def values(u):
                        t, hd = divmod(u, 4)
                        n = 1 if t == 0 else 3
                        p = (pA, pB)[u % 2]
                        pe.wait_ge(s_w, u + 1)
                        if u >= 2:
                            pe.wait_ge(s_o, u - 1)
                        for j in range(n):
                            last = nc.tensor.transpose(ps[:, 4 + u % 2, 128 * j:128 * j + 128], p[:, 0, 128 * j:128 * j + 128], ident)
                        last.then_inc(s_wtp, 1)
                        pe.wait_ge(s_wT, u + 1)
                        hc = slice(128 * hd, 128 * hd + 128)
                        vs = [vt[:, 0, hc]] if t == 0 else [cv[:, hc], vt[:, 1, hc], vt[:, 2, hc]]
                        for j in range(n):
                            last = mm(ps[:, 4 + u % 2, 384:512], wT[:, u % 2, 128 * j:128 * j + 128], vs[j], j == 0, j == n - 1)
                        last.then_inc(s_pv, 1)

                    pe.wait_ge(s_aT, 7)
                    scores(0)
                    for u in range(12):
                        if u + 1 < 12:
                            scores(u + 1)
                        for q in range(3 * u // 2, 3 * (u + 1) // 2):
                            plain(q, PLAIN_BANKS[0])
                        values(u)
                    pe.wait_ge(s_p, 24)
                    pe.wait_ge(s_conv, 1)
                    for t in range(TB):
                        c0 = 0 if t == 0 else ZS - PAD + 128 * (t - 1)
                        for cc in range(4):
                            last = nc.tensor.transpose(ps[:, t, 128 * cc:128 * cc + 128], conv[:, cc, c0:c0 + 128], ident)
                        last.then_inc(s_ztp, 1)

                    def cat_ready(t):
                        if t == 0:
                            pe.wait_ge(s_zn, 3)
                            pe.wait_ge(s_on, 1)
                            pe.wait_ge(s_o, 12)
                        pe.wait_ge(s_zs, t + 1)
                    transposes(cat, 1, cat_ready)
                    pe.wait_ge(s_tl, 12)
                    project(WOUT, 0)
                else:
                    pe.wait_ge(s_h, 9)
                    pe.wait_ge(s_pev, 36)
                    pe.wait_ge(s_dft, 16)

                    def stage1(q):
                        if q:
                            pe.wait_ge(s_Pa, 2 * q)
                            pe.wait_ge(s_Pd, 2 * q)
                        for jj in range(2):
                            dc = slice(256 * q + 128 * jj, 256 * q + 128 * jj + 128)
                            mm(ps[:, 2 * jj, 0:256], h[:, 0, dc], dftt[:, 0:256], True, True)
                            mm(ps[:, 2 * jj + 1, :], h[:, 1, dc], dftt[:, 256:768], True, False)
                            last = mm(ps[:, 2 * jj + 1, :], h[:, 2, dc], dftt[:, 768:1280], False, True)
                        last.then_inc(s_s1, 1)

                    def stage2(q):
                        pe.wait_ge(s_Pa, 2 * q + 2)
                        pe.wait_ge(s_Pd, 2 * q + 2)
                        if q >= 2:
                            pe.wait_ge(s_fl, 2 * (q - 1))
                        for oc in range(2):
                            out = ps[:, 4 + 2 * (q % 2) + oc, 0:TOK]
                            for jj in range(2):
                                for s, o in ((0, 1280), (1, 1792)):
                                    w = dftt[:, o + 256 * jj + 128 * oc:o + 256 * jj + 128 * oc + 128]
                                    last = mm(out, w, P[:, q % 2, jj, TOK * s:TOK * s + TOK], jj + s == 0, jj + s == 2)
                        last.then_inc(s_s2, 1)

                    stage1(0)
                    for q in range(4):
                        if q < 3:
                            stage1(q + 1)
                        stage2(q)
                    pe.wait_ge(s_fl, 8)
                    project(WF, 4)
                if l == 0:
                    for q in range(*SEG[0]):
                        plain(q, PLAIN_BANKS[1])
                    pe.wait_ge(s_pev, SEG[0][1])
                transposes(h, 2 + l, lambda t: (pe.wait_ge(s_h, 6 * l + 4 + t), pe.wait_ge(s_yo, 4 * l + 4)))
                pe.wait_ge(s_tl, 18 + 6 * l)
                pe.wait_ge(s_wrl, l + 1)
                for k in range(8):
                    mm(ps[0:20, 6, 0:TOK], wrl[:, k, :], hTl[:, k, :], k == 0, False)
                    last = mm3(ps[0:20, 6, 0:TOK], wrh[:, k, :], wrl[:, k, :], hTh[:, k, :], hTl[:, k, :], False, k == 7)
                last.then_inc(s_lgT, 1)
                pe.wait_ge(s_lgc, l + 1)
                for t in range(TB):
                    last = nc.tensor.transpose(ps[:, 6, 20 * t:20 * t + 20], lgT[0:20, 128 * t:128 * t + 128], cst[0:20, 0:20])
                last.then_inc(s_lg, 1)
                if l == 0:
                    for q in range(*SEG[1]):
                        plain(q, PLAIN_BANKS[2])
                pe.wait_ge(s_sel, l + 1)
                tri, one = cst[:, C_TRI:C_TRI + 128], cst[:, C_ONE:C_ONE + 128]
                sel = rt[:, 320:368]
                mm(ps[:, 7, 0:48], tri, sel, True, True)
                last = mm(ps[:, 7, 48:96], one, sel, True, True)
                last.then_inc(s_cum, 1)
                if l == 0:
                    for q in range(*SEG[2]):
                        plain(q, PLAIN_BANKS[2])
                    pe.wait_ge(s_pev, SEG[2][1])

                def x_transposes():
                    v = xg[:].rearrange("p (c k) -> p k c", k=8)
                    for k in range(8):
                        last = nc.tensor.transpose(ps[:, k // 4, 128 * (k % 4):128 * (k % 4) + 128], v[:, k, :], ident)
                    last.then_inc(s_xtp, 1)

                base = MOE0 if l == 0 else MOE1
                pe.wait_ge(s_xg, 16 * (17 * l + 1))
                x_transposes()
                with pe.Fori(0, NE) as e:
                    pe.wait_ge(s_xtl, e * 2 + (34 * l + 2))
                    for u in range(4):
                        wait_unit(base + u, e)
                        wh, wl = unit(base + u, 4)
                        for k in range(4):
                            kk = 4 * (u % 2) + k
                            last = mm3(ps[:, 2 + u // 2, :], hTh[:, kk, 0:128], hTl[:, kk, 0:128], wh[:, k, :], wl[:, k, :],
                                       kk == 0, kk == 7)
                        last.then_inc(s_unit, 1)
                    pe.wait_ge(s_xg, e * 16 + 16 * (17 * l + 2))
                    x_transposes()
                    pe.wait_ge(s_hid, e + (16 * l + 1))
                    v = hid[:].rearrange("p (c k) -> p k c", k=4)
                    for k in range(4):
                        last = nc.tensor.transpose(ps[:, 4, 128 * k:128 * k + 128], v[:, k, :], ident)
                    last.then_inc(s_htp, 1)
                    pe.wait_ge(s_htl, e + (16 * l + 1))
                    for u in range(4, 6):
                        wait_unit(base + u, e)
                        wh, wl = unit(base + u, 2)
                        for k in range(2):
                            kk = 2 * (u - 4) + k
                            for o in range(2):
                                last = mm3(ps[:, 5 + o, :], hTh[:, kk, 128:256], hTl[:, kk, 128:256],
                                           wh[:, k, 512 * o:512 * o + 512], wl[:, k, 512 * o:512 * o + 512], kk == 0, kk == 3)
                        last.then_inc(s_unit, 1)

                O = OV[l]
                pe.wait_ge(s_mx, l + 1)
                cnt = pe.value_load(mxi[0:1, 0:1], min_val=0, max_val=TOK)
                with pe.If(cnt > 128):
                    for b in (1, 2):
                        with pe.Fori(0, NE) as e:
                            n0 = NE * (b - 1)
                            pe.wait_ge(O["g"], e * 16 + 16 * (n0 + 1))
                            v = xg[:].rearrange("p (c k) -> p k c", k=8)
                            for k in range(8):
                                last = nc.tensor.transpose(ps[:, k // 4, 128 * (k % 4):128 * (k % 4) + 128], v[:, k, :], ident)
                            last.then_inc(O["tp"], 1)
                            pe.wait_ge(O["xt"], e + (n0 + 1))
                            for u in range(6):
                                if u == 4:
                                    pe.wait_ge(O["hid"], e + (n0 + 1))
                                    v = hid[:].rearrange("p (c k) -> p k c", k=4)
                                    for k in range(4):
                                        last = nc.tensor.transpose(ps[:, 4, 128 * k:128 * k + 128], v[:, k, :], ident)
                                    last.then_inc(O["htp"], 1)
                                    pe.wait_ge(O["ht"], e + (n0 + 1))
                                pe.wait_ge(O["w"][u % 2], e * 48 + 16 * (3 * n0 + u // 2 + 1))
                                if u < 4:
                                    w = wov[:, u % 2, :].rearrange("p (k n) -> p k n", k=4)
                                    for k in range(4):
                                        kk = 4 * (u % 2) + k
                                        last = mm(ps[:, 2 + u // 2, :], xTo[:, kk, :], w[:, k, :], kk == 0, kk == 7)
                                else:
                                    w = wov[:, u % 2, :].rearrange("p (k n) -> p k n", k=2)
                                    for k in range(2):
                                        kk = 2 * (u - 4) + k
                                        for o in range(2):
                                            last = mm(ps[:, 5 + o, :], hTo[:, kk, :], w[:, k, 512 * o:512 * o + 512], kk == 0, kk == 3)
                                last.then_inc(O["u"], 1)
                if l == 0:
                    for q in range(27, 36):
                        plain(q, PLAIN_BANKS[1])

        def overflow_act(act, l):
            O = OV[l]
            act.wait_ge(s_mx, l + 1)
            cnt = act.value_load(mxi[0:1, 0:1], min_val=0, max_val=TOK)
            with act.If(cnt > 128):
                for b in (1, 2):
                    with act.Fori(0, NE) as e:
                        n0 = NE * (b - 1)
                        act.wait_ge(O["tp"], e + (n0 + 1))
                        for j in range(2):
                            last = nc.scalar.activation(xTo[:, 4 * j:4 * j + 4, :],
                                                        ps[:, j, :].rearrange("p (k n) -> p k n", k=4), ACT.Copy)
                        last.then_inc(O["xt"], 1)
                        act.wait_ge(O["u"], e * 6 + (6 * n0 + 4))
                        nc.scalar.activation(sg[:], ps[:, 2, :], ACT.Silu).then_inc(O["sg"], 1)
                        act.wait_ge(O["htp"], e + (n0 + 1))
                        nc.scalar.activation(hTo[:], ps[:, 4, :].rearrange("p (k n) -> p k n", k=4), ACT.Copy).then_inc(O["ht"], 1)
                        act.wait_ge(O["u"], e * 6 + (6 * n0 + 6))
                        for o in range(2):
                            nc.scalar.activation(yrow[:, 512 * o:512 * o + 512], ps[:, 5 + o, :], ACT.Copy).then_inc(O["y"], 1)

        @block.scalar
        def _(act):
            def split(g, i=None):
                n = 16 * (ring(g) // RAW + 1)
                act.wait_ge(s_raw[ring(g) % RAW], n if i is None else i * 16 + n)
                if g >= SPL:
                    act.wait_ge(s_unit, g - SPL + 1 if i is None else i * 6 + (g - SPL + 1))
                nc.scalar.activation(H[:, g % SPL, :], raw[:, ring(g) % RAW, :], ACT.Copy).then_inc(s_hi, 1)

            def squares(added=None, beside=None):
                for t in range(TB):
                    if added is not None:
                        act.wait_ge(s_gu, added + t + 1)
                    if beside:
                        beside(t)
                    nc.scalar.activation(h[:, t, :], y[:, t, :], ACT.Square, accum_out=small[:, t:t + 1]).then_inc(s_sq, 1)

            def t_hi(r):
                for t in range(TB):
                    act.wait_ge(s_tp, 3 * r + t + 1)
                    for b in range(2):
                        nc.scalar.activation(hTh[:, 4 * b:4 * b + 4, 128 * t:128 * t + 128],
                                             ps[:, 2 * t + b, :].rearrange("p (k n) -> p k n", k=4), ACT.Copy).then_inc(s_th, 1)

            def f_hi(q):
                act.wait_ge(s_s2, q + 1)
                for oc in range(2):
                    nc.scalar.activation(hTh[:, 2 * q + oc, :], ps[:, 4 + 2 * (q % 2) + oc, 0:TOK], ACT.Copy).then_inc(s_fh, 1)

            act.dma_start(cT[:, 0, :], c_ctx.rearrange("(p k) -> p k", p=128)).then_inc(s_cT, 16)
            act.dma_start(cT[:, 1, :], c[0].rearrange("(p k) -> p k", p=128)).then_inc(s_cT, 16)
            act.dma_start(cst[:], consts).then_inc(s_cst, 16)
            def router_in(l):
                act.dma_start(wr[:, :, 0:4], w_router_group[l].rearrange("(p k) n -> p k n", p=128)).then_inc(s_wrin, 16)
                act.dma_start(wr[:, :, 4:20], w_router_expert[l].rearrange("(p k) n -> p k n", p=128)).then_inc(s_wrin, 16)
            act.wait_ge(s_cT, 32)
            nc.scalar.activation(cS[:].rearrange("p k c -> p c k"), cT[:], ACT.Silu).then_inc(s_sil, 1)
            act.wait_ge(s_sil, 1)
            nc.scalar.activation(cH[:], cS[:], ACT.Copy).then_inc(s_sil, 1)
            for g in range(SPL):
                split(g)
            with act.Fori(0, 2) as i:
                for u in range(6):
                    split(MOD0 + SPL + u, i)
            act.wait_ge(s_cwt, 1)
            nc.scalar.activation(cw[:].rearrange("p a b -> p (a b)"), ps[:, 7, 0:128], ACT.Copy).then_inc(s_cw, 1)

            def rows(q, banks):
                act.wait_ge(s_plain, q + 1)
                if q >= 2:
                    act.wait_ge(s_mxs[q % 2], 16 * (q // 2))
                nc.scalar.activation(mrow2[0:2, q % 2, :], ps[0:2, banks[q % 2], 0:256], ACT.Copy).then_inc(s_pev, 1)
                act.wait_ge(s_pev, q + 1)
                act.dma_start(modx[q // 12, :, 256 * (q % 12):256 * (q % 12) + 256], mrow2[0:2, q % 2, :]).then_inc(s_mxs[q % 2], 16)

            def keep_rows(q, part, banks):
                act.wait_ge(s_plain, q + 1)
                c0 = 256 * (q - PLAIN_0[part])
                nc.scalar.activation(mrow_p[part - 1][0:2, c0:c0 + 256], ps[0:2, banks[q % 2], 0:256], ACT.Copy).then_inc(s_pev, 1)

            def store_rows(q0, q1, part, stored):
                act.wait_ge(s_pev, q1)
                c0 = 256 * (q0 - PLAIN_0[part])
                act.dma_start(modx[q0 // 12, :, 256 * (q0 % 12):256 * (q0 % 12 + q1 - q0)],
                              mrow_p[part - 1][0:2, c0:c0 + 256 * (q1 - q0)]).then_inc(stored, 16)

            for l in range(2):
                if l == 0:
                    act.wait_ge(s_yin, 16 * 13)
                    act.wait_ge(s_mrow, 1)
                    squares()
                    act.wait_ge(s_lam, 1)
                    nc.scalar.activation(lams[:, 2:4], lams[:, 0:2], ACT.Exp).then_inc(s_le, 1)
                    router_in(0)
                    t_hi(0)
                    for j in range(4):
                        if j % 2 == 0:
                            act.wait_ge(s_unit, WIN + j + 1)
                            if j:
                                act.wait_ge(s_z, 2)
                            nc.scalar.activation(sig[:], ps[:, 0:2, 0:TOK], ACT.Sigmoid).then_inc(s_sig, 1)
                        split(WIN + j + SPL)
                    for j in range(6):
                        act.wait_ge(s_unit, WIN + 4 + j + 1)
                        if j < 4:
                            dst = h[:, :, 256 * j:256 * j + 256]
                        else:
                            dst = vt[:, :, 256 * (j - 4):256 * (j - 4) + 256]
                        b = 4 * (j % 2)
                        nc.scalar.activation(dst, ps[:, b:b + 3, 0:256], ACT.Copy).then_inc(s_qkv, 1)
                        if j < 3:
                            split(WIN + 4 + j + SPL)
                    dsts = [kT[:, :, 0:128], qT[:, :, 0:128], kT[:, :, 128:256], kT[:, :, 256:384], kT[:, :, 384:512],
                            qT[:, :, 128:256], qT[:, :, 256:384]]
                    for j, dst in enumerate(dsts):
                        act.wait_ge(s_atp, j + 1)
                        nc.scalar.activation(dst, ps[:, j, :].rearrange("p (k n) -> p k n", k=4), ACT.Copy).then_inc(s_aT, 1)

                    def exps(u):
                        nk = 128 if u < 4 else 384
                        act.wait_ge(s_nm, u + 1)
                        if u >= 2:
                            act.wait_ge(s_wtp, u - 1)
                        for cc in range(2):
                            nc.scalar.activation((pA, pB)[u % 2][:, cc, 0:nk], ps[:, 2 * (u % 2) + cc, 0:nk], ACT.Exp,
                                                 bias=small[:, 64 + 2 * u + cc:65 + 2 * u + cc], scale=0.125,
                                                 accum_out=small[:, 88 + 2 * u + cc:89 + 2 * u + cc]).then_inc(s_p, 1)

                    exps(0)
                    for u in range(12):
                        t, hd = divmod(u, 4)
                        n = 128 if t == 0 else 384
                        if u + 1 < 12:
                            exps(u + 1)
                        for q in range(3 * u // 2, 3 * (u + 1) // 2):
                            rows(q, PLAIN_BANKS[0])
                        act.wait_ge(s_wtp, u + 1)
                        if u >= 2:
                            act.wait_ge(s_pv, u - 1)
                        nc.scalar.activation(wT[:, u % 2, 0:n], ps[:, 4 + u % 2, 0:n], ACT.Copy).then_inc(s_wT, 1)
                        act.wait_ge(s_pv, u + 1)
                        dst = cat[:, t, 512 + 128 * hd:640 + 128 * hd]
                        nc.scalar.activation(dst, ps[:, 4 + u % 2, 384:512], ACT.Square,
                                             accum_out=small[:, 12 + u:13 + u]).then_inc(s_ach, 1)
                        act.wait_ge(s_ach, u + 1)
                        nc.scalar.activation(dst, ps[:, 4 + u % 2, 384:512], ACT.Copy).then_inc(s_o, 1)
                    for j in range(SPL):
                        split(WOUT + j)
                    for t in range(TB):
                        act.wait_ge(s_zn, t + 1)
                        nc.scalar.activation(cat[:, t, 0:512], cat[:, t, 0:512], ACT.Silu).then_inc(s_zs, 1)
                    t_hi(1)
                    split(WOUT + 3)
                else:
                    router_in(1)
                    squares(0, beside=lambda t: keep_rows(31 + t, 2, PLAIN_BANKS[1]))
                    for q in range(34, 36):
                        keep_rows(q, 2, PLAIN_BANKS[1])
                    store_rows(27, 36, 2, s_mx3[1])
                    for j in range(SPL):
                        split(WF + j)
                    for q in range(4):
                        act.wait_ge(s_s1, q + 1)
                        for jj in range(2):
                            nc.scalar.activation(
                                P[:, q % 2, jj, :].rearrange("p (s n) -> p s n", s=2)[:, :, 128:384],
                                ps[:, 2 * jj + 1, :].rearrange("p (s n) -> p s n", s=2), ACT.Copy).then_inc(s_Pa, 1)
                        if q:
                            f_hi(q - 1)
                    f_hi(3)
                    for j in range(4):
                        split(WF + j + SPL)
                act.wait_ge(s_y, 2 * l + 1)
                act.wait_ge(s_kv, 32)
                squares()
                if l == 0:
                    for q in range(*SEG[0]):
                        keep_rows(q, 1, PLAIN_BANKS[1])
                act.wait_ge(s_wrin, 32 * (l + 1))
                nc.scalar.activation(wrh[:], wr[:], ACT.Copy).then_inc(s_wrh, 1)
                t_hi(2 + l)
                act.wait_ge(s_lgT, l + 1)
                nc.scalar.activation(lgT[0:20, :], ps[0:20, 6, 0:TOK], ACT.Copy).then_inc(s_lgc, 1)
                act.wait_ge(s_rg, l + 1)
                nc.scalar.activation(rt[:, 72:84], rt[:, 60:72], ACT.Exp).then_inc(s_re, 1)
                act.wait_ge(s_rd, l + 1)
                nc.scalar.activation(rt[:, 303:306], rt[:, 300:303], ACT.Exp).then_inc(s_re2, 1)

                if l == 0:
                    for q in range(SEG[1][0], SEG[2][1]):
                        keep_rows(q, 1, PLAIN_BANKS[2])
                    store_rows(18, 24, 1, s_mx2)
                    store_rows(24, 27, 1, s_mx3[0])
                    for u in range(SPL):
                        split(MOE0 + u)

                def x_hi(v):
                    act.wait_ge(s_xtp, v)
                    for b in range(2):
                        nc.scalar.activation(hTh[:, 4 * b:4 * b + 4, 0:128],
                                             ps[:, b, :].rearrange("p (k n) -> p k n", k=4), ACT.Copy).then_inc(s_xth, 1)

                base = MOE0 if l == 0 else MOE1
                x_hi(v=17 * l + 1)

                def expert(e, more):
                    nc.scalar.activation(small[:, 159:160], cst[:, C_ONE:C_ONE + 1], ACT.Silu).then_inc(s_ach, 1)

                    def sp_(u):
                        if more or u < 3:
                            split(base + u + SPL, e)
                    sp_(0)
                    sp_(1)
                    act.wait_ge(s_unit, e * 6 + (base + 2))
                    nc.scalar.activation(sg[:], ps[:, 2, :], ACT.Silu).then_inc(s_sg, 1)
                    sp_(2)
                    x_hi(v=e + (17 * l + 2))
                    act.wait_ge(s_htp, e + (16 * l + 1))
                    nc.scalar.activation(hTh[:, 0:4, 128:256], ps[:, 4, :].rearrange("p (k n) -> p k n", k=4),
                                         ACT.Copy).then_inc(s_hth, 1)
                    sp_(3)
                    sp_(4)
                    act.wait_ge(s_unit, e * 6 + (base + 6))
                    for o in range(2):
                        nc.scalar.activation(yrow[:, 512 * o:512 * o + 512], ps[:, 5 + o, :], ACT.Copy).then_inc(s_yev, 1)
                    sp_(5)

                with act.Fori(0, NE - 1) as e:
                    expert(e, True)
                expert(NE - 1, False)
                overflow_act(act, l)
                if l == 0:
                    for q in range(27, 31):
                        keep_rows(q, 2, PLAIN_BANKS[1])
            squares(3)
            for t in range(TB):
                act.wait_ge(s_h, 12 + t + 1)
                dst = y_prompt[0] if t == 0 else y_sample[0, 128 * (t - 1):128 * t, :]
                act.dma_start(dst, h[:, t, :]).then_inc(s_out, 16)
            act.wait_ge(s_out, 48)

        def route(dve, link, l):
            V = nc.vector

            def b3(x, w):
                return x.unsqueeze(2).to_broadcast([128, 3, w])

            def bc(lo, w):
                return cst[:, lo:lo + w].unsqueeze(1).to_broadcast([128, 3, w])

            def v(lo, w):
                return rt[:, lo:lo + 3 * w].rearrange("p (t w) -> p t w", t=3)

            def first_max(d, consts, w, tmp, mn, out):
                link(V.scalar_tensor_tensor(out=tmp, in0=d, scalar=0.0, in1=bc(consts, w), op0=ALU.is_equal, op1=ALU.mult))
                link(V.tensor_reduce(out=mn, in_=tmp, axis=AX.X, op=ALU.min))
                link(V.tensor_tensor(out, bc(consts, w), b3(mn, w), ALU.is_equal))

            lg, gs, eg, tg, ohg, mg = v(0, 20), v(60, 4), v(72, 4), v(84, 4), v(96, 4), v(108, 4)
            gmax, sumg, gp, mn = rt[:, 120:123], rt[:, 123:126], rt[:, 126:129], rt[:, 129:132]
            ml, d, oh1, sel, oh2, ml2, pos, t16 = (v(132, 16), v(180, 16), v(228, 16), v(320, 16), v(368, 16), v(416, 16),
                                                  v(464, 16), v(512, 16))
            m1, m2 = rt[:, 276:279], rt[:, 279:282]
            dm, r, w1, w2, rp = rt[:, 300:303], rt[:, 303:306], rt[:, 306:309], rt[:, 309:312], rt[:, 312:315]
            df, gt, mx = rt[:, 560:566], rt[:, 640:691], rt[:, 700:701]
            dve.wait_ge(s_lg, l + 1)
            link(V.tensor_tensor(lg, ps[:, 6, 0:60].rearrange("p (t w) -> p t w", t=3),
                                 brt[:, l, :].unsqueeze(1).to_broadcast([128, 3, 20]), ALU.add))
            link(V.tensor_reduce(out=gmax, in_=lg[:, :, 0:4], axis=AX.X, op=ALU.max))
            V.tensor_tensor(gs, lg[:, :, 0:4], b3(gmax, 4), ALU.subtract).then_inc(s_rg, 1)
            dve.wait_ge(s_rg, l + 1)
            first_max(gs, C_J4, 4, tg, mn, ohg)
            link(V.tensor_scalar(mg, ohg, 1e30, -1e30, ALU.mult, ALU.add))
            ml4 = rt[:, 132:180].rearrange("p (t g e) -> p t g e", t=3, g=4)

            def ge(x):
                return x.unsqueeze(3).to_broadcast([128, 3, 4, 4])
            link(V.tensor_tensor(ml4, lg[:, :, 4:20].rearrange("p t (g e) -> p t g e", g=4), ge(ohg), ALU.mult))
            link(V.tensor_tensor(ml4, ml4, ge(mg), ALU.add))
            link(V.tensor_reduce(out=m1, in_=ml, axis=AX.X, op=ALU.max))
            link(V.tensor_tensor(d, ml, b3(m1, 16), ALU.subtract))
            first_max(d, C_J16, 16, t16, mn, oh1)
            link(V.scalar_tensor_tensor(out=ml2, in0=oh1, scalar=-3e30, in1=ml, op0=ALU.mult, op1=ALU.add))
            link(V.tensor_reduce(out=m2, in_=ml2, axis=AX.X, op=ALU.max))
            V.tensor_tensor(dm, m2, m1, ALU.subtract).then_inc(s_rd, 1)
            link(V.tensor_tensor(d, ml2, b3(m2, 16), ALU.subtract))
            first_max(d, C_J16, 16, t16, mn, oh2)
            V.tensor_tensor(sel, oh1, oh2, ALU.add).then_inc(s_sel, 1)
            dve.wait_ge(s_re, l + 1)
            link(V.tensor_reduce(out=sumg, in_=eg, axis=AX.X, op=ALU.add))
            dve.wait_ge(s_re2, l + 1)
            link(V.tensor_scalar(rp, r, 1.0, None, ALU.add))
            link(V.tensor_tensor(rp, rp, sumg, ALU.mult))
            link(V.reciprocal(w1, rp))
            link(V.tensor_tensor(w2, w1, r, ALU.mult))
            dve.wait_ge(s_cum, l + 1)
            link(V.memset(rt[:, 592:640], 0.0))
            sums = [rt[:, 592:616], rt[:, 616:640]]
            cnt, c01, tot = v(512, 16), rt[:, 416:432], rt[:, 432:448]
            link(V.tensor_copy(cnt, ps[:, 7, 48:96].rearrange("p (t w) -> p t w", t=3)))
            link(V.tensor_tensor(c01, cnt[:, 0, :], cnt[:, 1, :], ALU.add))
            link(V.tensor_tensor(tot, c01, cnt[:, 2, :], ALU.add))
            link(V.tensor_copy(sums[0][:, 8:24], tot))
            for i, k in enumerate((1, 2, 4, 8)):
                a, b = sums[i % 2], sums[1 - i % 2]
                link(V.tensor_tensor(b[:, 8:24], a[:, 8:24], a[:, 8 - k:24 - k], ALU.add))
            off = sums[1][:, 8:24]
            link(V.tensor_tensor(off, sums[0][:, 8:24], tot, ALU.subtract))
            link(V.tensor_tensor(pos, ps[:, 7, 0:48].rearrange("p (t w) -> p t w", t=3),
                                 off.unsqueeze(1).to_broadcast([128, 3, 16]), ALU.add))
            link(V.tensor_tensor(pos[:, 1, :], pos[:, 1, :], cnt[:, 0, :], ALU.add))
            link(V.tensor_tensor(pos[:, 2, :], pos[:, 2, :], c01, ALU.add))
            for k, oh in enumerate((oh1, oh2)):
                link(V.tensor_tensor(t16, pos, oh, ALU.mult))
                link(V.tensor_reduce(out=df[:, 3 * k:3 * k + 3], in_=t16, axis=AX.X, op=ALU.add))
            V.tensor_copy(di[:, 0:6], df).then_inc(s_route, 1)
            link(V.memset(gt, 0.0))
            for b in range(3):
                link(V.tensor_scalar(gt[:, 17 * b:17 * b + 16], tot, cst[:, C_P + b:C_P + b + 1], BIG,
                                     ALU.is_le, ALU.mult))
            gt3 = gt.rearrange("p (b e) -> p b e", b=3)[:, :, 0:16]
            link(V.tensor_tensor(gt3, gt3, off.unsqueeze(1).to_broadcast([128, 3, 16]), ALU.add))
            link(V.tensor_tensor(gtab[:, 0:51], gt, cst[:, C_EP:C_EP + 51], ALU.add))
            link(V.tensor_reduce(out=mx, in_=tot, axis=AX.X, op=ALU.max))
            V.tensor_copy(mxi[:, 0:1], mx).then_inc(s_mx, 1)
            dve.wait_ge(s_mx, l + 1)

        @block.vector
        def _(dve):
            n = [0]

            def link(ins):
                n[0] += 1
                ins.then_inc(s_dch, 1)
                dve.wait_ge(s_dch, n[0])

            def rest(g, i=None):
                dve.wait_ge(s_hi, g + 1 if i is None else i * 6 + (g + 1))
                nc.vector.tensor_tensor(L[:, g % SPL, :], raw[:, ring(g) % RAW, :], H[:, g % SPL, :].bitcast(f32),
                                        ALU.subtract).then_inc(s_lo, 1)

            def t_lo(r):
                for j in range(6):
                    dve.wait_ge(s_th, 6 * r + j + 1)
                    t, b = divmod(j, 2)
                    hs = (slice(None), slice(4 * b, 4 * b + 4), slice(128 * t, 128 * t + 128))
                    nc.vector.tensor_tensor(hTl[hs], ps[:, j, :].rearrange("p (k n) -> p k n", k=4),
                                            hTh[hs].bitcast(f32), ALU.subtract).then_inc(s_tl, 1)

            def mod():
                dve.wait_ge(s_bmod, 16)
                for u in range(12):
                    dve.wait_ge(s_unit, MOD0 + u + 1)
                    col = slice(256 * u, 256 * u + 256)
                    nc.vector.tensor_tensor(modrow[0:2, col], ps[0:2, u % 6, 0:256], bmod[0:2, col], ALU.add).then_inc(s_mev, 1)
                    if u < 12 - SPL:
                        rest(MOD0 + SPL + u)
                dve.wait_ge(s_mev, 12)
                dve.wait_ge(s_gn, 16)
                r = modrow[0:2, D:2 * D]
                nc.vector.scalar_tensor_tensor(out=r, in0=r, scalar=1.0, in1=gn[0:2, :], op0=ALU.add, op1=ALU.mult).then_inc(s_mrow, 1)
                for u in range(SPL):
                    rest(WIN + u)

            def norm(j):
                dve.wait_ge(s_rstd, j + 1)
                dve.wait_ge(s_par, 32 * (j + 1))
                for t in range(TB):
                    cond = min(t, 1)
                    link(nc.vector.scalar_tensor_tensor(out=h[:, t, :], in0=y[:, t, :], scalar=small[:, 3 + t:4 + t],
                                                        in1=par[:, 1, cond, :], op0=ALU.mult, op1=ALU.mult))
                    nc.vector.tensor_tensor(h[:, t, :], h[:, t, :], par[:, 0, cond, :], ALU.add).then_inc(s_h, 1)

            def project(g0):
                dve.wait_ge(s_gate, 16 if g0 == WOUT else 48)
                for j in range(4):
                    dve.wait_ge(s_unit, g0 + j + 1)
                    c0 = slice(256 * j, 256 * j + 256)
                    for t in range(TB):
                        ins = nc.vector.tensor_tensor(tmp3[:, t, :], ps[:, 4 * (j % 2) + t, 0:256], par[:, 2, min(t, 1), c0], ALU.mult)
                        if t < 2:
                            ins.then_inc(s_dch, 1)
                            n[0] += 1
                        else:
                            ins.then_inc(s_yo, 1)
                    dve.wait_ge(s_dch, n[0])
                    dve.wait_ge(s_yo, (0 if g0 == WOUT else 4) + j + 1)
                    link(nc.vector.tensor_tensor(y[:, :, c0], y[:, :, c0], tmp3[:], ALU.add))
                    if j == 3:
                        nc.vector.memset(rt[:, 719:720], 0.0).then_inc(s_y, 1)
                    if g0 == WF or j == 0:
                        rest(g0 + j + SPL)

            dve.wait_ge(s_sil, 2)
            nc.vector.tensor_tensor(cL[:], cS[:], cH[:].bitcast(f32), ALU.subtract).then_inc(s_cs, 1)
            for g in range(SPL):
                rest(g)
            for l in range(2):
                if l == 0:
                    mod()
                    dve.wait_ge(s_yin, 16 * 13)
                    for i in range(2):
                        last = nc.vector.scalar_tensor_tensor(out=rt[:, 64 * i:64 * i + 64], in0=lamv[:, 2 * i, :], scalar=1.0,
                                                              in1=lamv[:, 2 * i + 1, :], op0=ALU.mult, op1=ALU.mult,
                                                              accum_out=lams[:, i:i + 1])
                    last.then_inc(s_lam, 1)
                    norm(0)
                    t_lo(0)
                    dve.wait_ge(s_zp, 1)
                    for j in range(4):
                        if j % 2:
                            i = j // 2
                            dve.wait_ge(s_unit, WIN + j + 1)
                            dve.wait_ge(s_sig, i + 1)
                            for a, b, o in ((0, 128, PAD), (128, 384, ZS)):
                                nc.vector.tensor_tensor(zpad[:, 2 * i:2 * i + 2, o:o + b - a], ps[:, 2:4, a:b], sig[:, :, a:b],
                                                        ALU.mult).then_inc(s_z, 1)
                        rest(WIN + j + SPL)
                    for j in range(3):
                        rest(WIN + 4 + j + SPL)
                    cn = [0]
                    dve.wait_ge(s_cw, 1)
                    dve.wait_ge(s_le, 1)
                    link(nc.vector.tensor_tensor(lams[:, 4:5], lams[:, 3:4], lams[:, 2:3], ALU.subtract))
                    link(nc.vector.tensor_scalar(lams[:, 5:6], lams[:, 4:5], -0.2, None, ALU.add))
                    dve.wait_ge(s_z, 4)

                    def taps(t0, t1):
                        for tap in range(t0, t1):
                            if tap:
                                dve.wait_ge(s_tap, 4 * tap)
                            for cc in range(4):
                                src = zpad[:, cc, tap:tap + CL]
                                if tap == 0:
                                    ins = nc.vector.tensor_scalar(conv[:, cc, :], src, cw[:, cc, 0:1], cw[:, cc, 31:32],
                                                                  ALU.mult, ALU.add)
                                else:
                                    ins = nc.vector.scalar_tensor_tensor(out=conv[:, cc, :], in0=src, scalar=cw[:, cc, tap:tap + 1],
                                                                         in1=conv[:, cc, :], op0=ALU.mult, op1=ALU.add)
                                ins.then_inc(s_tap, 1)

                    def neg_max(u):
                        nk = 128 if u < 4 else 384
                        dve.wait_ge(s_sc, u + 1)
                        b = 2 * (u % 2)
                        link(nc.vector.tensor_reduce(out=small[:, 112 + 2 * u:114 + 2 * u], in_=ps[:, b:b + 2, 0:nk], axis=AX.X,
                                                     op=ALU.max, negate=True))
                        nc.vector.tensor_scalar(small[:, 64 + 2 * u:66 + 2 * u], small[:, 112 + 2 * u:114 + 2 * u], 0.125, None,
                                                ALU.mult).then_inc(s_nm, 1)

                    taps(0, FIRST)
                    neg_max(0)
                    for u in range(12):
                        nk = 128 if u < 4 else 384
                        if u + 1 < 12:
                            neg_max(u + 1)
                        p = (pA, pB)[u % 2]
                        dve.wait_ge(s_p, 2 * u + 2)
                        rs = small[:, 136 + 2 * u:138 + 2 * u]
                        link(nc.vector.reciprocal(rs, small[:, 88 + 2 * u:90 + 2 * u]))
                        link(nc.vector.tensor_scalar(rs[:, 1:2], rs[:, 1:2], lams[:, 5:6], None, ALU.mult))
                        link(nc.vector.tensor_scalar(p[:, 0, 0:nk], p[:, 0, 0:nk], rs[:, 0:1], None, ALU.mult))
                        nc.vector.scalar_tensor_tensor(out=p[:, 0, 0:nk], in0=p[:, 1, 0:nk], scalar=rs[:, 1:2],
                                                       in1=p[:, 0, 0:nk], op0=ALU.mult, op1=ALU.add).then_inc(s_w, 1)
                        taps(FIRST + (TAPS - FIRST) * u // 12, FIRST + (TAPS - FIRST) * (u + 1) // 12)
                    dve.wait_ge(s_tap, 4 * TAPS)
                    nc.vector.memset(rt[:, 718:719], 0.0).then_inc(s_conv, 1)
                    for t in range(TB):
                        dve.wait_ge(s_ztp, t + 1)
                        link(nc.vector.bn_stats(rt[:, 6 * t:6 * t + 6], ps[:, t, :]))
                        nc.vector.bn_aggr(small[:, 48 + 2 * t:50 + 2 * t], rt[:, 6 * t:6 * t + 6]).then_inc(s_zv, 1)
                    link(nc.vector.tensor_scalar(sub[:], sub[:], 1.0 - LAM_INIT, None, ALU.mult))
                    dve.wait_ge(s_rso, 1)
                    for u in range(12):
                        t, hd = divmod(u, 4)
                        x = cat[:, t, 512 + 128 * hd:640 + 128 * hd]
                        last = nc.vector.scalar_tensor_tensor(out=x, in0=x, scalar=small[:, 24 + u:25 + u], in1=sub[:],
                                                              op0=ALU.mult, op1=ALU.mult)
                    last.then_inc(s_on, 1)
                    dve.wait_ge(s_zv, 3)
                    dve.wait_ge(s_rsz, 1)
                    for t in range(TB):
                        z = cat[:, t, 0:512]
                        link(nc.vector.tensor_scalar(z, ps[:, t, :], small[:, 48 + 2 * t:49 + 2 * t], small[:, 57 + t:58 + t],
                                                     ALU.subtract, ALU.mult))
                        link(nc.vector.tensor_tensor(z, z, lnb[:, 0, :], ALU.mult))
                        nc.vector.tensor_tensor(z, z, lnb[:, 1, :], ALU.add).then_inc(s_zn, 1)
                    rest(WOUT)
                    t_lo(1)
                    rest(WOUT + 1)
                    rest(WOUT + 2)
                    dve.wait_ge(s_kv, 32)
                    project(WOUT)
                else:
                    norm(2)
                    for j in range(SPL):
                        rest(WF + j)
                    dve.wait_ge(s_mx3[1], 16)
                    for q in range(4):
                        dve.wait_ge(s_s1, q + 1)
                        for jj in range(2):
                            nc.vector.tensor_copy(
                                P[:, q % 2, jj, :].rearrange("p (s n) -> p s n", s=2)[:, :, 0:128],
                                ps[:, 2 * jj, 0:256].rearrange("p (s n) -> p s n", s=2)).then_inc(s_Pd, 1)
                        for f in ([q - 1] if q else []) + ([3] if q == 3 else []):
                            for oc in range(2):
                                dve.wait_ge(s_fh, 2 * f + oc + 1)
                                nc.vector.tensor_tensor(hTl[:, 2 * f + oc, :], ps[:, 4 + 2 * (f % 2) + oc, 0:TOK],
                                                        hTh[:, 2 * f + oc, :].bitcast(f32), ALU.subtract).then_inc(s_fl, 1)
                    project(WF)
                norm(2 * l + 1)
                dve.wait_ge(s_wrh, l + 1)
                nc.vector.tensor_tensor(wrl[:], wr[:], wrh[:].bitcast(f32), ALU.subtract).then_inc(s_wrl, 1)
                t_lo(2 + l)
                route(dve, link, l)
                nc.vector.tensor_copy(gix[:, 0:1], gtab[:, 0:1]).then_inc(s_gi, 1)
                if l == 0:
                    for u in range(SPL):
                        rest(MOE0 + u)

                base = MOE0 if l == 0 else MOE1

                def x_lo(v):
                    for b in range(2):
                        dve.wait_ge(s_xth, v * 2 + (b - 1))
                        nc.vector.tensor_tensor(hTl[:, 4 * b:4 * b + 4, 0:128], ps[:, b, :].rearrange("p (k n) -> p k n", k=4),
                                                hTh[:, 4 * b:4 * b + 4, 0:128].bitcast(f32), ALU.subtract).then_inc(s_xtl, 1)

                def index(dst, col, done=None):
                    ins = nc.vector.tensor_copy(dst[:, 0:1], gtab[:, ds(col, 1)])
                    if done is not None:
                        ins.then_inc(done, 1)

                def expert(e, more):
                    def rest_(u):
                        if more or u < 3:
                            rest(base + u + SPL, e)
                    for u in range(3):
                        rest_(u)
                    dve.wait_ge(s_sg, e + (16 * l + 1))
                    dve.wait_ge(s_unit, e * 6 + (base + 4))
                    nc.vector.tensor_tensor(hid[:], ps[:, 3, :], sg[:], ALU.mult).then_inc(s_hid, 1)
                    x_lo(e + (17 * l + 2))
                    index(gix, e + 2, s_gi)
                    dve.wait_ge(s_ysc, e * 16 + 16 * (16 * l + 1))
                    index(six, e)
                    dve.wait_ge(s_hth, e + (16 * l + 1))
                    nc.vector.tensor_tensor(hTl[:, 0:4, 128:256], ps[:, 4, :].rearrange("p (k n) -> p k n", k=4),
                                            hTh[:, 0:4, 128:256].bitcast(f32), ALU.subtract).then_inc(s_htl, 1)
                    for u in range(3, 6):
                        rest_(u)

                x_lo(17 * l + 1)
                nc.vector.tensor_copy(gix[:, 0:1], gtab[:, 1:2]).then_inc(s_gi, 1)
                with dve.Fori(0, NE - 1) as e:
                    expert(e, True)
                expert(NE - 1, False)
                O = OV[l]
                cnt = dve.value_load(mxi[0:1, 0:1], min_val=0, max_val=TOK)
                with dve.If(cnt > 128):
                    for b in (1, 2):
                        if b == 1:
                            dve.wait_ge(s_gi, 18 * (l + 1))
                        if b == 2:
                            dve.wait_ge(O["i"], 17)
                        nc.vector.tensor_copy(gix[:, 0:1], gtab[:, 17 * b:17 * b + 1]).then_inc(O["i"], 1)
                        with dve.Fori(0, NE) as e:
                            dve.wait_ge(O["sg"], e + (NE * (b - 1) + 1))
                            nc.vector.tensor_tensor(hid[:], ps[:, 3, :], sg[:], ALU.mult).then_inc(O["hid"], 1)
                            dve.wait_ge(O["st"], e * 16 + 16 * (NE * (b - 1) + 1))
                            index(gix, e + (17 * b + 1), O["i"])
                dve.wait_ge(s_gate, 32 * (l + 1))
                for t in range(TB):
                    dve.wait_ge(s_ga[t], 32 * (l + 1))
                    ga, gb = pairs[t]
                    link(nc.vector.tensor_scalar(ga[:], ga[:], rt[:, 306 + t:307 + t], None, ALU.mult))
                    link(nc.vector.scalar_tensor_tensor(out=gb[:], in0=gb[:], scalar=rt[:, 309 + t:310 + t], in1=ga[:],
                                                        op0=ALU.mult, op1=ALU.add))
                    link(nc.vector.tensor_tensor(gb[:], gb[:], par[:, 2, min(t, 1), :], ALU.mult))
                    nc.vector.tensor_tensor(y[:, t, :], y[:, t, :], gb[:], ALU.add).then_inc(s_gu, 1)
                dve.wait_ge(s_gu, 3 * l + 3)
                nc.vector.memset(rt[:, 719:720], 0.0).then_inc(s_y, 1)
            dve.wait_ge(s_par, 144)
            for t in range(TB):
                dve.wait_ge(s_rstd, 4 + t + 1)
                nc.vector.scalar_tensor_tensor(out=h[:, t, :], in0=y[:, t, :], scalar=small[:, 3 + t:4 + t],
                                               in1=par[:, 0, 0, :], op0=ALU.mult, op1=ALU.mult).then_inc(s_h, 1)


FIRST = 11
PLAIN_BANKS = ((6, 7), (7, 3), (5, 3))
SEG = ((18, 21), (21, 22), (22, 27))
LAM_INIT = 0.8 - 0.6
_INS = ["x_prompt", "x_sample", "cache_k", "cache_v", "c", "c_ctx", "w_mod", "b_mod", "norm1_g", "norm2_g", "w_in_even",
        "conv_w", "conv_b", "conv_ln_g", "conv_ln_b", "lambda_q1", "lambda_k1", "lambda_q2", "lambda_k2", "subln_g",
        "w_out_even", "w_fnet", "w_router_group", "b_router_group", "w_router_expert", "b_router_expert",
        "w_gate_exp", "w_up_exp", "w_down_exp", "final_norm_g"]
_OUTS = [(1, 128, 1024), (1, 256, 1024), (1, 1, 128, 4, 128), (1, 1, 128, 4, 128)]


def kernel(**inputs):
    import numpy as _np
    import concourse.bacc as _bacc
    from concourse import mybir as _mybir
    from concourse.bass_utils import run_bass_kernel_spmd as _run

    nc = _bacc.Bacc("TRN2", target_bir_lowering=False, num_devices=1)
    arrays, args = {}, []
    shaped = {"consts": constants(), "dft": dft_tables()}
    for name in _INS + ["consts", "dft"]:
        a = _np.ascontiguousarray(inputs[name] if name in inputs else shaped[name])
        arrays[f"in_{name}"] = a
        args.append(nc.dram_tensor(f"in_{name}", a.shape, _mybir.dt.from_np(a.dtype), kind="ExternalInput").ap())
    for i, shape in enumerate(_OUTS):
        args.append(nc.dram_tensor(f"out_{i}", shape, _mybir.dt.float32, kind="ExternalOutput").ap())
    build(nc, *args)
    r = _run(nc, [arrays], core_ids=[0])
    return tuple(r.results[0][f"out_{i}"] for i in range(4))
```
